# Optimizing a Trainium2 kernel written in Bass

```python
import jax, jax.numpy as jnp
from jax import lax
import numpy as np

D_MODEL = 1024
BATCH = 1
SEQ = 1024
DEPTH = 1

MEM_LEN = 256
MIX_WIDTH = D_MODEL
SGU_WIDTH = MIX_WIDTH // 2
SGU_GROUPS = 4
SGU_GROUP_DIM = SGU_WIDTH // SGU_GROUPS
CHUNK = 128
SB_WIDTH = MIX_WIDTH - SGU_WIDTH
SB_HEAD_DIM = 64
SB_HEADS = SB_WIDTH // SB_HEAD_DIM
Q_BLOCK = 128
XA_HEADS = 4
XA_HEAD_DIM = D_MODEL // XA_HEADS
D_FF = ((8 * D_MODEL // 3 + 127) // 128) * 128
IN_COLS = 2 * SGU_WIDTH + 3 * SB_WIDTH
EPS = 1e-6

kernel_name = "hybrid_sgu_stickbreaking_macaron_block"

def rmsnorm(x, g):
    xf = x.astype(jnp.float32)
    y = xf * lax.rsqrt(jnp.mean(xf * xf, axis=-1, keepdims=True) + EPS)
    return (y * g.astype(jnp.float32)).astype(x.dtype)

def swiglu(x, w_gate, w_up, w_down):
    return (jax.nn.silu(x @ w_gate) * (x @ w_up)) @ w_down

def chunked_sgu(u, v, norm_g, norm_b, w_s, b_s):
    B, S, G, Dg = v.shape
    vf = v.astype(jnp.float32)
    mu = jnp.mean(vf, axis=-1, keepdims=True)
    var = jnp.mean((vf - mu) ** 2, axis=-1, keepdims=True)
    vn = ((vf - mu) * lax.rsqrt(var + EPS) * norm_g.astype(jnp.float32)
          + norm_b.astype(jnp.float32)).astype(v.dtype)
    vc = vn.reshape(B, S // CHUNK, CHUNK, G, Dg)
    causal = jnp.tril(jnp.ones((CHUNK, CHUNK), dtype=bool))
    w = jnp.where(causal[None], w_s, jnp.zeros_like(w_s)).astype(v.dtype)
    mixed = jnp.einsum('gts,bcsgd->bctgd', w, vc) + b_s.T.astype(v.dtype)[None, None, :, :, None]
    return u * mixed.reshape(B, S, G, Dg)

def stick_breaking_attention(q, k, v):
    B, H, S, Dh = q.shape
    scale = Dh ** -0.5
    outs = []
    for blk in range(S // Q_BLOCK):
        t0 = blk * Q_BLOCK
        t1 = t0 + Q_BLOCK
        qb = q[:, :, t0:t1]
        kb = k[:, :, :t1]
        vb = v[:, :, :t1]
        z = jnp.einsum('bhtd,bhsd->bhts', qb, kb,
                       preferred_element_type=jnp.float32) * scale
        t_idx = t0 + jnp.arange(Q_BLOCK)[:, None]
        s_idx = jnp.arange(t1)[None, :]
        strict = s_idx < t_idx
        log_beta = jax.nn.log_sigmoid(z)
        log_1m = jnp.where(strict, jax.nn.log_sigmoid(-z), 0.0)
        suffix = lax.cumsum(log_1m, axis=log_1m.ndim - 1, reverse=True) - log_1m
        a = jnp.where(strict, jnp.exp(log_beta + suffix), 0.0)
        outs.append(jnp.einsum('bhts,bhsd->bhtd', a.astype(v.dtype), vb))
    return jnp.concatenate(outs, axis=2)

def memory_cross_attention(x, memn, w_q, w_kv, w_o):
    B, S, D = x.shape
    M = memn.shape[1]
    q = (x @ w_q).reshape(B, S, XA_HEADS, XA_HEAD_DIM)
    kv = (memn @ w_kv).reshape(B, M, 2, XA_HEADS, XA_HEAD_DIM)
    k, v = kv[:, :, 0], kv[:, :, 1]
    logits = jnp.einsum('bshd,bmhd->bhsm', q, k,
                        preferred_element_type=jnp.float32) * (XA_HEAD_DIM ** -0.5)
    p = jax.nn.softmax(logits, axis=-1).astype(v.dtype)
    o = jnp.einsum('bhsm,bmhd->bshd', p, v).reshape(B, S, XA_HEADS * XA_HEAD_DIM)
    return o @ w_o

def setup_inputs(seed: int = 0) -> dict:
    key = jax.random.key(seed)
    ks = iter(jax.random.split(key, 40))
    L, D, F = DEPTH, D_MODEL, D_FF

    def nrm(shape, scale):
        return jax.random.normal(next(ks), shape, jnp.float32) * scale

    def gain(shape):
        return 1.0 + nrm(shape, 0.02)

    return {
        "x": nrm((BATCH, SEQ, D), 1.0),
        "mem": nrm((BATCH, MEM_LEN, D), 1.0),
        "ffn1_pre_g": gain((L, D)),
        "ffn1_post_g": gain((L, D)),
        "ffn1_w_gate": nrm((L, D, F), D ** -0.5),
        "ffn1_w_up": nrm((L, D, F), D ** -0.5),
        "ffn1_w_down": nrm((L, F, D), F ** -0.5),
        "mix_pre_g": gain((L, D)),
        "mix_post_g": gain((L, D)),
        "w_in": nrm((L, D, IN_COLS), D ** -0.5),
        "sgu_norm_g": gain((L, SGU_GROUPS, SGU_GROUP_DIM)),
        "sgu_norm_b": nrm((L, SGU_GROUPS, SGU_GROUP_DIM), 0.02),
        "sgu_w_s": nrm((L, SGU_GROUPS, CHUNK, CHUNK), CHUNK ** -0.5),
        "sgu_b_s": 1.0 + nrm((L, SGU_GROUPS, CHUNK), 0.02),
        "sgu_out_g": gain((L, SGU_WIDTH)),
        "sb_out_g": gain((L, SB_WIDTH)),
        "w_out": nrm((L, MIX_WIDTH, D), MIX_WIDTH ** -0.5),
        "xa_pre_g": gain((L, D)),
        "xa_post_g": gain((L, D)),
        "mem_norm_g": gain((L, D)),
        "xa_w_q": nrm((L, D, XA_HEADS * XA_HEAD_DIM), D ** -0.5),
        "xa_w_kv": nrm((L, D, 2 * XA_HEADS * XA_HEAD_DIM), D ** -0.5),
        "xa_w_o": nrm((L, XA_HEADS * XA_HEAD_DIM, D), (XA_HEADS * XA_HEAD_DIM) ** -0.5),
        "ffn2_pre_g": gain((L, D)),
        "ffn2_post_g": gain((L, D)),
        "ffn2_w_gate": nrm((L, D, F), D ** -0.5),
        "ffn2_w_up": nrm((L, D, F), D ** -0.5),
        "ffn2_w_down": nrm((L, F, D), F ** -0.5),
        "final_norm_g": gain((L, D)),
    }

def reference(x, mem, ffn1_pre_g, ffn1_post_g, ffn1_w_gate, ffn1_w_up, ffn1_w_down,
              mix_pre_g, mix_post_g, w_in, sgu_norm_g, sgu_norm_b, sgu_w_s, sgu_b_s,
              sgu_out_g, sb_out_g, w_out, xa_pre_g, xa_post_g, mem_norm_g, xa_w_q,
              xa_w_kv, xa_w_o, ffn2_pre_g, ffn2_post_g, ffn2_w_gate, ffn2_w_up,
              ffn2_w_down, final_norm_g):
    B, S, D = x.shape
    splits = [SGU_WIDTH, 2 * SGU_WIDTH, 2 * SGU_WIDTH + SB_WIDTH,
              2 * SGU_WIDTH + 2 * SB_WIDTH]
    h = x
    for l in range(DEPTH):
        f = swiglu(rmsnorm(h, ffn1_pre_g[l]), ffn1_w_gate[l], ffn1_w_up[l], ffn1_w_down[l])
        h = h + 0.5 * rmsnorm(f, ffn1_post_g[l])

        n = rmsnorm(h, mix_pre_g[l])
        proj = n @ w_in[l]
        u, vg, q, k, vs = jnp.split(proj, splits, axis=-1)
        u = jax.nn.gelu(u).reshape(B, S, SGU_GROUPS, SGU_GROUP_DIM)
        vg = jax.nn.gelu(vg).reshape(B, S, SGU_GROUPS, SGU_GROUP_DIM)
        out_a = chunked_sgu(u, vg, sgu_norm_g[l], sgu_norm_b[l],
                            sgu_w_s[l], sgu_b_s[l]).reshape(B, S, SGU_WIDTH)

        def heads(t):
            return t.reshape(B, S, SB_HEADS, SB_HEAD_DIM).transpose(0, 2, 1, 3)
        out_b = stick_breaking_attention(heads(q), heads(k), heads(vs))
        out_b = out_b.transpose(0, 2, 1, 3).reshape(B, S, SB_WIDTH)

        merged = jnp.concatenate([rmsnorm(out_a, sgu_out_g[l]),
                                  rmsnorm(out_b, sb_out_g[l])], axis=-1)
        h = h + rmsnorm(merged @ w_out[l], mix_post_g[l])

        c = memory_cross_attention(rmsnorm(h, xa_pre_g[l]), rmsnorm(mem, mem_norm_g[l]),
                                   xa_w_q[l], xa_w_kv[l], xa_w_o[l])
        h = h + rmsnorm(c, xa_post_g[l])

        f = swiglu(rmsnorm(h, ffn2_pre_g[l]), ffn2_w_gate[l], ffn2_w_up[l], ffn2_w_down[l])
        h = h + 0.5 * rmsnorm(f, ffn2_post_g[l])

        h = rmsnorm(h, final_norm_g[l])
    return h


_drawn_inputs = setup_inputs


def setup_inputs(seed=0):
    import zlib

    import numpy as np

    out = dict(_drawn_inputs(seed))
    spreads = {}
    factors = {'ffn1_pre_g': 3.788,
     'ffn1_post_g': 5.889,
     'mix_pre_g': 3.41,
     'mix_post_g': 4.324,
     'sgu_norm_g': 8.0,
     'sgu_norm_b': 22.224,
     'sgu_b_s': 7.769,
     'sgu_out_g': 6.225,
     'sb_out_g': 5.747,
     'xa_pre_g': 5.025,
     'xa_post_g': 19.06,
     'mem_norm_g': 3.277,
     'ffn2_pre_g': 86.186,
     'ffn2_post_g': 176.425,
     'final_norm_g': 20.539}
    for name, (base, spread) in spreads.items():
        noise = np.random.default_rng([zlib.crc32(name.encode()), seed]).standard_normal(out[name].shape)
        drawn = base * np.exp(spread * noise) if base else spread * noise
        out[name] = __import__('jax').numpy.asarray(drawn.astype(out[name].dtype))
    for name, factor in factors.items():
        out[name] = (out[name] * factor).astype(out[name].dtype)
    return out
```

```python
from contextlib import ExitStack

import concourse.bass as bass
from concourse import mybir

ACT = mybir.ActivationFunctionType
ALU = mybir.AluOpType
AX = mybir.AxisListType
F32 = mybir.dt.float32
F32R = mybir.dt.float32r
BF16 = mybir.dt.bfloat16

P = 128
BANK = 512
EPS = 1e-6
MASKED = -1e30


class Uses:

    def __init__(self):
        self.n = [0, 0, 0]


def build(nc, a, out):
    S, D = a["x"].shape[1:]
    M = a["mem"].shape[1]
    FF = a["ffn1_w_gate"].shape[2]
    G, CH = a["sgu_w_s"].shape[1:3]
    SW = a["sgu_out_g"].shape[1]
    GD = SW // G
    SBW = a["sb_out_g"].shape[1]
    HD = 64
    SBH = SBW // HD
    XH_HEADS = 4
    XHD = D // XH_HEADS
    NT = S // P
    NK = D // P
    NM = M // P
    NF = FF // P
    CHUNKS = NF // 2
    PAIRS = NT // 2
    SLOT = 2 * D
    HALF = S // 2
    assert S == D == 1024 and NF % 2 == 0 and CH == P and GD == P and HALF == BANK

    ctx = ExitStack()
    with ctx:
        def sem(name):
            return ctx.enter_context(nc.semaphore(name))

        def Sems(stage, *names):
            return {n: sem(f"{stage}_{n}") for n in names}

        def sb(name, shape, dt=F32):
            return ctx.enter_context(nc.sbuf_tensor(name, shape, dt))

        w_raw = sb("w_raw", [P, 3, SLOT])
        w_hi = sb("w_hi", [P, 3, SLOT], F32R)
        w_lo = sb("w_lo", [P, 3, SLOT], F32R)
        ident = sb("ident", [P, P])
        causal_neg = sb("causal_neg", [P, P])
        square_out = sb("square_out", [P, D], BF16)
        sums = sb("sums", [P, 2 * NT])
        rstd = sb("rstd", [P, 2 * NT])
        half_pow = sb("half_pow", [P, 8])
        small = sb("small", [P, 96])

        def overlay(*tensors):
            with ExitStack() as place:
                return [place.enter_context(nc.sbuf_tensor(n, shape, dt)) for n, shape, dt in tensors]

        sb_work = overlay(
            ("beta", [P, 2, S], F32), ("keep", [P, 2, S], F32), ("suffix", [P, 2, S + 8], F32),
            ("attn_t", [P, 2, S], F32))
        beta, keep, suffix, attn_t = sb_work
        x_hi = sb("x_hi", [P, NK, S], F32R)
        x_lo = sb("x_lo", [P, NK, S], F32R)

        u_sb, q_t, v_sb, k_t = overlay(
            ("u_sb", [P, NT, SW], F32), ("q_t", [P, SBW // P, S], F32), ("v_sb", [P, NT, SBW], F32),
            ("k_t", [P, SBW // P, S], F32))
        _, vg, vn, _, _, sgu_bc, ws_raw, ws_t = overlay(
            ("o_u", [P, NT, SW], F32), ("vg", [P, 2, SW], F32), ("vn", [P, 2, SW], F32),
            ("o_q", [P, 2048], F32), ("o_v", [P, NT, SBW], F32),
            ("sgu_bc", [P, 2, SW], F32), ("ws_raw", [P, G, P], F32), ("ws_t", [P, G, P], F32))
        xq_t, probs, probs_t, _, mk_t, mv = overlay(
            ("xq_t", [P, NK, S], F32), ("probs", [P, 2, XH_HEADS, M], F32), ("probs_t", [P, D], F32),
            ("o_x", [P, 1024], F32), ("mk_t", [P, NK, M], F32), ("mv", [P, NM, D], F32))
        m_hi, m_lo = overlay(("m_hi", [P, NK, M], F32R), ("m_lo", [P, NK, M], F32R))
        y = sb("y", [P, NT, D])
        hid_hi, hid_lo = overlay(("hid_hi", [P, 2, S], F32R), ("hid_lo", [P, 2, S], F32R))
        resid = sb("resid", [P, 2, D])
        normed = sb("normed", [P, 2, D])
        gate_act = sb("gate_act", [P, 2, HALF])
        product = sb("product", [P, 2, HALF])
        gain_post = sb("gain_post", [P, D])
        gain_pre = sb("gain_pre", [P, D])

        ps = ctx.enter_context(nc.psum_tensor("ps", [P, 8, BANK], F32))

        def bank(b, n=1):
            return ps[:, b:b + n, :].rearrange("p b c -> p (b c)")

        h_dram = [nc.dram_tensor(f"h_scratch{i}", [S, D], F32, kind="Internal").ap() for i in range(3)]
        x_in = a["x"][0]

        raw_full = [sem(f"raw_full{s}") for s in range(3)]
        hi_done = [sem(f"hi_done{s}") for s in range(3)]
        w_full = [sem(f"w_full{s}") for s in range(3)]
        const = Sems("const", "zero", "made")
        mean_square = sem("mean_square")

        PRE = ("gain_pre", "sum_h", "rstd_h", "normed")
        POST = ("gain_post", "sum_y", "rstd_y", "scaled", "h")
        TURN = ("turned", "x_hi", "x_full")
        norm0 = Sems("norm0", *PRE, *TURN)
        norm1 = Sems("norm1", *POST, *PRE, *TURN, "stored")
        norm_merge = Sems("normm", *PRE, *TURN, "sum_y", "rstd_y")
        norm2 = Sems("norm2", *POST, *PRE, *TURN, "stored")
        norm3 = Sems("norm3", *POST, *PRE, *TURN, "stored")
        norm4 = Sems("norm4", *POST, *PRE)
        norm_mem = Sems("normx", *PRE, *TURN)
        resid_full = [sem(f"resid_full{u}") for u in range(2)]
        for s, n in ((norm0, 0), (norm1, NT), (norm2, 2 * NT), (norm_mem, 3 * NT), (norm3, 3 * NT + NM),
                     (norm4, 4 * NT + NM)):
            s["loads"] = n // 2

        def wait_resid(eng, s, t):
            eng.wait_ge(resid_full[t % 2], 16 * (s["loads"] + t // 2 + 1))

        FFN = ("gu", "gate_act", "product", "hid_hi", "hid_full", "down", "y")
        ffn = Sems("ffn", *FFN)
        mix = Sems("mix", "uv_half", "uv", "u", "vg", "stats", "rstd", "vn0", "vn1", "vn1b", "vn", "gated",
                   "out_a", "qk", "q", "const", "masked", "ws_turned", "ws", "v_half", "v", "v_done")
        sb_att = Sems("sb", "ones", "z", "beta", "keep", "diag", "suffix", "attn", "turned", "attn_t", "av", "out_b")
        wout = Sems("wout", "half", "full", "y")
        xkv = Sems("xkv", "k", "k_done", "half", "v", "v_done")
        xq = Sems("xq", "q", "q_done")
        xatt = Sems("xatt", "logits", "max", "neg", "probs", "recip", "scaled", "turned", "probs_t", "o", "o_hi", "o_full")
        xo = Sems("xo", "half", "full", "y")
        stored_out = [sem(f"stored_out{u}") for u in range(2)]

        block = ctx.enter_context(nc.Block())

        def split3(pe, dst, lh, ll, rh, rl, first, last):
            pe.matmul(dst, lh, rh, start=first, stop=False)
            pe.matmul(dst, lh, rl, start=False, stop=False)
            return pe.matmul(dst, ll, rh, start=False, stop=last)

        def load_block(sp, uses, s, halves, it=0, steps=1):
            n = uses.n[s]
            if steps > 1 or not isinstance(it, int):
                sp.wait_ge(w_full[s], n + it)
            elif n:
                sp.wait_ge(w_full[s], n)
            for dst, src in halves:
                sp.dma_start(dst, src).then_inc(raw_full[s], 16)

        def block_cols(name, s, c0, width):
            w = a[name][0].rearrange("(k p) c -> p k c", p=P)
            dst = w_raw[:, s, :].rearrange("p (k c) -> p k c", c=width)
            h = NK // 2
            return [(dst[:, i * h:(i + 1) * h, :], w[:, i * h:(i + 1) * h, c0:c0 + width]) for i in range(2)]

        def block_rows(name, s, k0, c0):
            w = a[name][0].rearrange("(k p) c -> p k c", p=P)
            dst = w_raw[:, s, :].rearrange("p (k c) -> p k c", c=BANK)
            return [(dst[:, 2 * i:2 * i + 2, :], w[:, k0 + 2 * i:k0 + 2 * i + 2, c0:c0 + BANK]) for i in range(2)]

        def split_hi(act, s, n):
            act.wait_ge(raw_full[s], n * 32)
            act.activation(w_hi[:, s, :], w_raw[:, s, :], ACT.Copy).then_inc(hi_done[s], 1)

        def split_lo(dve, s, n):
            dve.wait_ge(hi_done[s], n)
            dve.tensor_tensor(w_lo[:, s, :], w_raw[:, s, :], w_hi[:, s, :].bitcast(F32),
                              ALU.subtract).then_inc(w_full[s], 1)

        def ffn_loads(sp, p, uses, it, first, last):
            gate = a[p + "_w_gate"][0].rearrange("(k p) c -> p k c", p=P)
            up = a[p + "_w_up"][0].rearrange("(k p) c -> p k c", p=P)
            down = a[p + "_w_down"][0].rearrange("(f p) c -> p f c", p=P)

            def gu(f, c, i):
                dst = w_raw[:, f, :].rearrange("p (g k c) -> p g k c", g=2, c=P)
                load_block(sp, uses, f, [(dst[:, 0], gate[:, :, bass.ds(c, P)]), (dst[:, 1], up[:, :, bass.ds(c, P)])], i)

            def dn(i):
                load_block(sp, uses, 2, [(w_raw[:, 2, f * D:(f + 1) * D], down[:, bass.ds(2 * i + f, 1), :]
                                          .rearrange("p f c -> p (f c)")) for f in range(2)], i)
            return gu, dn

        def ffn_pe(pe, s, uses, c0, x_full):
            def chunk(i, first):
                for f in range(2):
                    pe.wait_ge(w_full[f], uses.n[f] + 1 - c0 + i)
                    for h in range(2):
                        if not (first and f == 0):
                            pe.wait_ge(s["product"], 4 * i + 2 * f + h - 1)
                        if first and f == 0:
                            pe.wait_ge(x_full, NT // 2 * (h + 1))
                        for g in range(2):
                            for k in range(NK):
                                at = (g * NK + k) * P
                                mm = split3(pe, bank(2 * h + g), w_hi[:, f, at:at + P], w_lo[:, f, at:at + P],
                                            x_hi[:, k, h * HALF:(h + 1) * HALF], x_lo[:, k, h * HALF:(h + 1) * HALF],
                                            k == 0, k == NK - 1)
                            mm.then_inc(s["gu"], 1)
                pe.wait_ge(w_full[2], uses.n[2] + 1 - c0 + i)
                for t in range(NT):
                    if t % (NT // 2) == 0:
                        pe.wait_ge(s["hid_full"], 4 * i + 3 + t // (NT // 2))
                    for h in range(2):
                        n = 2 * t + h
                        if not (first and n < 4):
                            pe.wait_ge(s["y"], 16 * i + n - 3)
                        for f in range(2):
                            mm = split3(pe, bank(4 + n % 4), hid_hi[:, f, t * P:(t + 1) * P], hid_lo[:, f, t * P:(t + 1) * P],
                                        w_hi[:, 2, f * D + h * BANK:f * D + (h + 1) * BANK],
                                        w_lo[:, 2, f * D + h * BANK:f * D + (h + 1) * BANK], f == 0, f == 1)
                        mm.then_inc(s["down"], 1)
            chunk(c0, True)
            with pe.Fori(c0 + 1, c0 + CHUNKS) as i:
                chunk(i, False)
            for f in range(3):
                uses.n[f] += CHUNKS

        def ffn_act(act, s, uses, c0, prefetch_last):
            def hidden(i, f, h, first):
                idx = 4 * i + 2 * f + h
                act.wait_ge(s["gu"], 2 * idx + 1)
                if not (first and f == 0):
                    act.wait_ge(s["product"], idx - 1)
                act.activation(gate_act[:, h, :], bank(2 * h), ACT.Silu).then_inc(s["gate_act"], 1)
                act.wait_ge(s["product"], idx + 1)
                if not first:
                    act.wait_ge(s["down"], 16 * i)
                act.activation(hid_hi[:, f, h * HALF:(h + 1) * HALF], product[:, h, :], ACT.Copy).then_inc(s["hid_hi"], 1)

            def chunk(i, first, last):
                hidden(i, 0, 0, first)
                if not first:
                    act.wait_ge(s["down"], 16 * i)
                split_hi(act, 2, uses.n[2] + 1 - c0 + i)
                hidden(i, 0, 1, first)
                if not last:
                    act.wait_ge(s["gu"], 8 * i + 4)
                    split_hi(act, 0, uses.n[0] + 1 - c0 + i)
                hidden(i, 1, 0, first)
                hidden(i, 1, 1, first)
                if not last:
                    act.wait_ge(s["gu"], 8 * i + 8)
                    split_hi(act, 1, uses.n[1] + 1 - c0 + i)
            looped(act, chunk, c0, prefetch_last)
            uses.n[2] += CHUNKS
            for f in range(2):
                uses.n[f] += CHUNKS - (not prefetch_last)

        def looped(eng, chunk, c0, prefetch_last):
            chunk(c0, True, False)
            end = c0 + CHUNKS - (not prefetch_last)
            with eng.Fori(c0 + 1, end) as i:
                chunk(i, False, False)
            if not prefetch_last:
                chunk(end, False, True)

        def ffn_dve(dve, s, uses, c0, prefetch_last):
            def hidden(i, f, h):
                idx = 4 * i + 2 * f + h
                dve.wait_ge(s["gate_act"], idx + 1)
                dve.wait_ge(s["gu"], 2 * idx + 2)
                dve.tensor_tensor(product[:, h, :], gate_act[:, h, :], bank(2 * h + 1), ALU.mult).then_inc(s["product"], 1)
                dve.wait_ge(s["hid_hi"], idx + 1)
                at = slice(h * HALF, (h + 1) * HALF)
                dve.tensor_tensor(hid_lo[:, f, at], product[:, h, :], hid_hi[:, f, at].bitcast(F32),
                                  ALU.subtract).then_inc(s["hid_full"], 1)

            def chunk(i, first, last):
                hidden(i, 0, 0)
                split_lo(dve, 2, uses.n[2] + 1 - c0 + i)
                hidden(i, 0, 1)
                if not last:
                    split_lo(dve, 0, uses.n[0] + 1 - c0 + i)
                hidden(i, 1, 0)
                hidden(i, 1, 1)
                if not first:
                    dve.wait_ge(s["y"], 16 * i)
                for n in range(2 * NT):
                    t, h = n // 2, n % 2
                    dve.wait_ge(s["down"], 16 * i + n + 1)
                    acc = y[:, t, h * BANK:(h + 1) * BANK]
                    if first:
                        op = dve.tensor_copy(acc, bank(4 + n % 4))
                    else:
                        op = dve.tensor_tensor(acc, acc, bank(4 + n % 4), ALU.add)
                    op.then_inc(s["y"], 1)
                if not last:
                    split_lo(dve, 1, uses.n[1] + 1 - c0 + i)
            looped(dve, chunk, c0, prefetch_last)
            uses.n[2] += CHUNKS
            for f in range(2):
                uses.n[f] += CHUNKS - (not prefetch_last)

        def norm_loads(sp, s, resid_src, store, before_resid, tiles=NT):
            before_resid()
            for t in range(tiles):
                u = t % 2
                if t >= 2:
                    sp.wait_ge(s["normed"], t - 1)
                    if store is not None:
                        sp.wait_ge(s["stored"], 16 * (t - 1))
                sp.dma_start(resid[:, u, :], resid_src[t * P:(t + 1) * P, :]).then_inc(resid_full[u], 16)
                if store is not None and t >= 1:
                    sp.wait_ge(s["h"], t)
                    sp.dma_start(store[(t - 1) * P:t * P, :], resid[:, 1 - u, :]).then_inc(s["stored"], 16)
            if store is not None:
                sp.wait_ge(s["h"], tiles)
                sp.dma_start(store[(tiles - 1) * P:tiles * P, :], resid[:, 1, :]).then_inc(s["stored"], 16)

        def load_gain(sp, dst, src, done):
            sp.dma_start(dst, src.broadcast_to((P, src.shape[1]))).then_inc(done, 16)

        def norm_pe(pe, s, tiles, before):
            before()
            for t in range(tiles):
                u = t % 2
                pe.wait_ge(s["normed"], t + 1)
                if t >= 2:
                    pe.wait_ge(s["x_full"], t - 1)
                for k in range(NK):
                    mm = pe.transpose(bank(4 + 2 * u, 2)[:, k * P:(k + 1) * P], normed[:, u, k * P:(k + 1) * P], ident[:, :])
                mm.then_inc(s["turned"], 1)

        def mean_square_done(pool, op):
            squares[0] += 1
            op.then_inc(mean_square, 1)
            pool.wait_ge(mean_square, squares[0])

        squares = [0]

        def norm_pool(pool, s, which, n, width):
            ssum, done = (s["sum_y"], s["rstd_y"]) if which == "y" else (s["sum_h"], s["rstd_h"])
            col = n if which == "y" else NT + n
            pool.wait_ge(ssum, n + 1)
            mean_square_done(pool, pool.tensor_scalar(sums[:, col:col + 1], sums[:, col:col + 1], 1.0 / width, EPS,
                                                      ALU.mult, ALU.add))
            pool.tensor_tensor(rstd[:, col:col + 1], sums[:, col:col + 1], half_pow[:, 0:1], ALU.pow).then_inc(done, 1)

        def turn_act(act, s, t, hi):
            act.wait_ge(s["turned"], t + 1)
            act.activation(hi[:, :, t * P:(t + 1) * P], bank(4 + 2 * (t % 2), 2).rearrange("p (k c) -> p k c", c=P),
                           ACT.Copy).then_inc(s["x_hi"], 1)

        def turn_dve(dve, s, t, hi, lo):
            dve.wait_ge(s["x_hi"], t + 1)
            at = slice(t * P, (t + 1) * P)
            dve.tensor_tensor(lo[:, :, at], bank(4 + 2 * (t % 2), 2).rearrange("p (k c) -> p k c", c=P),
                              hi[:, :, at].bitcast(F32), ALU.subtract).then_inc(s["x_full"], 1)

        def norm_act(act, s, y_sem, y_at, post, x_free, last=None, tiles=NT):
            def square(src, col, done):
                act.activation(square_out[:, :], src, ACT.Square, accum_out=sums[:, col:col + 1]).then_inc(done, 1)
            for j in range(tiles // 2):
                for t in (2 * j, 2 * j + 1):
                    if post:
                        if t:
                            act.wait_ge(s["sum_h"] if t % 2 == 0 else s["sum_y"], t)
                        act.wait_ge(y_sem, y_at(t))
                        square(y[:, t, :], t, s["sum_y"])
                for t in (2 * j, 2 * j + 1):
                    if post:
                        act.wait_ge(s["sum_y"], 2 * j + 2)
                    if t:
                        act.wait_ge(s["sum_h"], t)
                    if post:
                        act.wait_ge(s["h"], t + 1)
                    else:
                        wait_resid(act, s, t)
                    square(resid[:, t % 2, :], NT + t, s["sum_h"])
                if last is None:
                    for t in (2 * j, 2 * j + 1):
                        if t == 0:
                            x_free(act)
                        turn_act(act, s, t, x_hi if tiles == NT else m_hi)

        def norm_dve(dve, s, c, post, last=None, tiles=NT):
            for j in range(tiles // 2):
                pair = (2 * j, 2 * j + 1)
                for t in pair:
                    if not post:
                        continue
                    u = t % 2
                    if t == 0:
                        dve.wait_ge(s["gain_post"], 16)
                    if t >= 2:
                        dve.wait_ge(s["turned"] if last is None else last[u], (t - 1) if last is None else 16 * (t // 2))
                    dve.wait_ge(s["rstd_y"], t + 1)
                    dve.scalar_tensor_tensor(normed[:, u, :], y[:, t, :], rstd[:, t:t + 1], gain_post[:, :],
                                             ALU.mult, ALU.mult).then_inc(s["scaled"], 1)
                for t in pair:
                    if not post:
                        continue
                    u = t % 2
                    dve.wait_ge(s["scaled"], t + 1)
                    wait_resid(dve, s, t)
                    dve.scalar_tensor_tensor(resid[:, u, :], normed[:, u, :], c, resid[:, u, :],
                                             ALU.mult, ALU.add).then_inc(s["h"], 1)
                for t in pair:
                    u = t % 2
                    if t == 0:
                        dve.wait_ge(s["gain_pre"], 16)
                    if not post and t >= 2:
                        dve.wait_ge(s["turned"], t - 1)
                    dve.wait_ge(s["rstd_h"], t + 1)
                    if post:
                        dve.wait_ge(s["h"], t + 1)
                    dve.scalar_tensor_tensor(normed[:, u, :], resid[:, u, :], rstd[:, NT + t:NT + t + 1], gain_pre[:, :],
                                             ALU.mult, ALU.mult).then_inc(s["normed"], 1)
                if last is None:
                    for t in pair:
                        turn_dve(dve, s, t, x_hi if tiles == NT else m_hi, x_lo if tiles == NT else m_lo)

        def norm_pool_all(pool, s, post, tiles=NT):
            for j in range(tiles // 2):
                if post:
                    for t in (2 * j, 2 * j + 1):
                        norm_pool(pool, s, "y", t, D)
                for t in (2 * j, 2 * j + 1):
                    norm_pool(pool, s, "h", t, D)

        def project_rows_pe(pe, uses, s_half, s_full, cb, tiles, src_hi, src_lo, bank_free):
            for s in range(2):
                pe.wait_ge(w_full[s], uses.n[s] + 1)
                for t in range(tiles):
                    if s == 0:
                        bank_free(t)
                    for k in range(4):
                        kk = 4 * s + k
                        mm = split3(pe, bank(t), src_hi[:, kk, t * P:(t + 1) * P], src_lo[:, kk, t * P:(t + 1) * P],
                                    w_hi[:, s, k * BANK:(k + 1) * BANK], w_lo[:, s, k * BANK:(k + 1) * BANK],
                                    s == 0 and k == 0, s == 1 and k == 3)
                    if s == 1:
                        mm.then_inc(s_full, 1)
                if s == 0:
                    mm.then_inc(s_half, 1)
                uses.n[s] += 1

        def project_cols_pe(pe, uses, s_full, s, n_cols, src_hi, src_lo, bank_free):
            pe.wait_ge(w_full[s], uses.n[s] + 1)
            halves = n_cols // BANK or 1
            width = min(n_cols, BANK)
            for c in range(2):
                for h in range(halves):
                    b = 4 * s + 2 * c + h
                    bank_free(b)
                    for k in range(NK):
                        at = k * 256 + c * P
                        mm = split3(pe, bank(b)[:, 0:width], w_hi[:, s, at:at + P], w_lo[:, s, at:at + P],
                                    src_hi[:, k, h * width:(h + 1) * width], src_lo[:, k, h * width:(h + 1) * width],
                                    k == 0, k == NK - 1)
                    mm.then_inc(s_full, 1)
            uses.n[s] += 1

        def next_hi(act, uses, s, ready, n):
            act.wait_ge(ready, n)
            uses.n[s] += 1
            split_hi(act, s, uses.n[s])

        def next_lo(dve, uses, s):
            uses.n[s] += 1
            split_lo(dve, s, uses.n[s])

        U_COLS, VG_COLS, Q_COLS = 0, SW, 2 * SW
        K_COLS, V_COLS = 2 * SW + SBW, 2 * SW + 2 * SBW
        out_b = q_t
        QK_BLOCKS = 2 * SBW // 256
        XK_BLOCKS = D // 256
        N_ATT = NT * SBH

        def att_step(n):
            return divmod(n, SBH)

        def o_hi_act(act, t):
            act.wait_ge(xatt["o"], t + 1)
            act.activation(x_hi[:, :, t * P:(t + 1) * P], bank(6, 2).rearrange("p (k c) -> p k c", c=P),
                           ACT.Copy).then_inc(xatt["o_hi"], 1)

        def gate_dve(dve, t):
            dve.wait_ge(mix["gated"], t + 1)
            if t == 0:
                dve.wait_ge(mix["u"], NT)
            for g in range(G):
                at = slice(g * GD, (g + 1) * GD)
                dve.scalar_tensor_tensor(u_sb[:, t, at], bank(t)[:, at], small[:, g:g + 1], u_sb[:, t, at],
                                         ALU.add, ALU.mult).then_inc(mix["out_a"], 1)

        def out_b_dve(dve, i):
            dve.wait_ge(sb_att["av"], SBH * (i + 1))
            dve.tensor_copy(out_b[:, :, i * P:(i + 1) * P], bank(6 + i % 2).rearrange("p (c d) -> p c d", d=P))\
               .then_inc(sb_att["out_b"], 1)

        def o_lo_dve(dve, t):
            dve.wait_ge(xatt["o_hi"], t + 1)
            at = slice(t * P, (t + 1) * P)
            dve.tensor_tensor(x_lo[:, :, at], bank(6, 2).rearrange("p (k c) -> p k c", c=P),
                              x_hi[:, :, at].bitcast(F32), ALU.subtract).then_inc(xatt["o_full"], 1)

        @block.sync
        def _(sp):
            uses = Uses()

            def one(s, halves):
                load_block(sp, uses, s, halves)
                uses.n[s] += 1

            load_gain(sp, gain_pre[:, :], a["ffn1_pre_g"], norm0["gain_pre"])
            norm_loads(sp, norm0, x_in, None, lambda: None, 2)
            gu, dn = ffn_loads(sp, "ffn1", uses, 0, True, False)
            for f in range(2):
                gu(f, f * P, 0)
                uses.n[f] += 1
            for t in range(2, NT):
                sp.wait_ge(norm0["normed"], t - 1)
                sp.dma_start(resid[:, t % 2, :], x_in[t * P:(t + 1) * P, :]).then_inc(resid_full[t % 2], 16)

            def ffn_rest(p, n_chunks):
                gu, dn = ffn_loads(sp, p, uses, 0, True, False)
                dn_n = uses.n[2]
                if dn_n:
                    sp.wait_ge(w_full[2], dn_n)
                down = a[p + "_w_down"][0].rearrange("(f p) c -> p f c", p=P)
                for f in range(2):
                    sp.dma_start(w_raw[:, 2, f * D:(f + 1) * D], down[:, f, :]).then_inc(raw_full[2], 16)
                with sp.Fori(1, n_chunks) as i:
                    for f in range(2):
                        gu(f, i * 2 * P + f * P, i - 1)
                    dn(i)
                uses.n[2] += n_chunks
                for f in range(2):
                    uses.n[f] += n_chunks - 1

            ffn_rest("ffn1", CHUNKS)
            def u_block(s, c0):
                one(s, block_rows("w_in", s, 4 * s, c0))
            for s in range(2):
                u_block(s, U_COLS)
            load_gain(sp, gain_post[:, :], a["ffn1_post_g"], norm1["gain_post"])
            sp.wait_ge(norm0["normed"], NT)
            load_gain(sp, gain_pre[:, :], a["mix_pre_g"], norm1["gain_pre"])
            sp.wait_ge(ffn["hid_full"], 4 * CHUNKS)
            load_gain(sp, sgu_bc[:, 0, :], a["sgu_norm_g"][0].rearrange("(o g) d -> o (g d)", o=1), mix["const"])
            load_gain(sp, sgu_bc[:, 1, :], a["sgu_norm_b"][0].rearrange("(o g) d -> o (g d)", o=1), mix["const"])
            sp.dma_start(ws_raw[:, :, :], a["sgu_w_s"][0].rearrange("g t s -> t g s")).then_inc(mix["const"], 16)
            sp.dma_start(small[:, 0:G], a["sgu_b_s"][0].rearrange("g t -> t g"),
                         allow_slow_non_contiguous=True).then_inc(mix["const"], 16)
            norm_loads(sp, norm1, x_in, h_dram[0], lambda: sp.wait_ge(ffn["down"], 16 * CHUNKS))
            for c0 in (VG_COLS, V_COLS):
                for s in range(2):
                    u_block(s, c0)
            for b in range(QK_BLOCKS):
                one(b % 2, block_cols("w_in", b % 2, Q_COLS + b * 256, 256))
            for s in range(2):
                one(s, block_rows("w_out", s, 4 * s, 0))
            sp.wait_ge(sb_att["z"], N_ATT)
            load_gain(sp, gain_pre[:, 0:SW], a["sgu_out_g"], norm_merge["gain_pre"])
            load_gain(sp, gain_pre[:, SW:D], a["sb_out_g"], norm_merge["gain_pre"])
            load_gain(sp, gain_post[:, :], a["mix_post_g"], norm2["gain_post"])
            for s in range(2):
                one(s, block_rows("w_out", s, 4 * s, BANK))
            for s in range(2):
                one(s, block_cols("xa_w_kv", s, s * 256, 256))
            sp.wait_ge(norm_merge["normed"], NT)
            load_gain(sp, gain_pre[:, :], a["xa_pre_g"], norm2["gain_pre"])
            sp.wait_ge(norm1["stored"], 16 * NT)
            norm_loads(sp, norm2, h_dram[0], h_dram[1], lambda: None)
            sp.wait_ge(norm2["normed"], NT)
            load_gain(sp, gain_pre[:, :], a["mem_norm_g"], norm_mem["gain_pre"])
            sp.wait_ge(norm2["stored"], 16 * NT)
            norm_loads(sp, norm_mem, a["mem"][0], None, lambda: None, NM)
            for b in range(2, XK_BLOCKS):
                one(b % 2, block_cols("xa_w_kv", b % 2, b * 256, 256))
            for cb in range(2):
                for s in range(2):
                    one(s, block_rows("xa_w_kv", s, 4 * s, D + cb * BANK))
            for b in range(XK_BLOCKS):
                one(b % 2, block_cols("xa_w_q", b % 2, b * 256, 256))
            for cb in range(2):
                for s in range(2):
                    one(s, block_rows("xa_w_o", s, 4 * s, cb * BANK))
            gu, dn = ffn_loads(sp, "ffn2", uses, 0, True, False)
            for f in range(2):
                gu(f, f * P, 0)
                uses.n[f] += 1
            sp.wait_ge(xatt["o_full"], NT)
            load_gain(sp, gain_post[:, :], a["xa_post_g"], norm3["gain_post"])
            load_gain(sp, gain_pre[:, :], a["ffn2_pre_g"], norm3["gain_pre"])
            norm_loads(sp, norm3, h_dram[1], h_dram[2], lambda: None)
            sp.wait_ge(norm3["stored"], 16 * NT)
            ffn_rest("ffn2", CHUNKS)
            load_gain(sp, gain_post[:, :], a["ffn2_post_g"], norm4["gain_post"])
            load_gain(sp, gain_pre[:, :], a["final_norm_g"], norm4["gain_pre"])
            sp.wait_ge(ffn["down"], 32 * CHUNKS)
            for t in range(NT):
                if t >= 2:
                    sp.wait_ge(norm4["normed"], t - 1)
                sp.dma_start(resid[:, t % 2, :], h_dram[2][t * P:(t + 1) * P, :]).then_inc(resid_full[t % 2], 16)
                if t >= 2:
                    sp.dma_start(out[0, (t - 2) * P:(t - 1) * P, :], normed[:, t % 2, :]).then_inc(stored_out[t % 2], 16)
            for t in (NT - 2, NT - 1):
                sp.wait_ge(norm4["normed"], t + 1)
                sp.dma_start(out[0, t * P:(t + 1) * P, :], normed[:, t % 2, :]).then_inc(stored_out[t % 2], 16)
            for u in range(2):
                sp.wait_ge(stored_out[u], 16 * PAIRS)

        @block.gpsimd
        def _(pool):
            pool.memset(half_pow[:, :], -0.5).then_inc(const["zero"], 1)
            pool.memset(ident[:, :], 0.0).then_inc(const["zero"], 1)
            pool.memset(causal_neg[:, :], 0.0).then_inc(const["zero"], 1)
            pool.wait_ge(const["zero"], 3)
            pool.affine_select(out=ident[:, :], in_=ident[:, :], compare_op=ALU.not_equal, fill=1.0, base=0,
                               pattern=[[-1, P]], channel_multiplier=1).then_inc(const["made"], 1)
            pool.affine_select(out=causal_neg[:, :], in_=causal_neg[:, :], compare_op=ALU.is_gt, fill=MASKED, base=0,
                               pattern=[[-1, P]], channel_multiplier=1).then_inc(const["made"], 1)
            norm_pool_all(pool, norm0, False)
            norm_pool_all(pool, norm1, True)
            pool.wait_ge(mix["const"], 64)
            pool.affine_select(out=ws_raw[:, :, :], in_=ws_raw[:, :, :], compare_op=ALU.is_ge, fill=0.0, base=0,
                               pattern=[[0, G], [-1, P]], channel_multiplier=1).then_inc(mix["masked"], 1)
            for t in range(NT):
                pool.wait_ge(mix["stats"], 4 * t + 4)
                v4 = small[:, 32 + 8 * (t % 2):40 + 8 * (t % 2)].rearrange("p (g two) -> p g two", two=2)
                mean_square_done(pool, pool.tensor_scalar(v4[:, :, 1], v4[:, :, 1], 1.0, EPS, ALU.mult, ALU.add))
                pool.tensor_tensor(v4[:, :, 1], v4[:, :, 1], half_pow[:, 0:4], ALU.pow).then_inc(mix["rstd"], 1)
            for t in range(NT):
                norm_pool(pool, norm_merge, "y", t, SW)
                norm_pool(pool, norm_merge, "h", t, SBW)
            norm_pool_all(pool, norm2, True)
            norm_pool_all(pool, norm_mem, False, NM)
            norm_pool_all(pool, norm3, True)
            norm_pool_all(pool, norm4, True)

        @block.scalar
        def _(act):
            uses = Uses()

            def nxt(s, ready, n):
                next_hi(act, uses, s, ready, n)

            norm_act(act, norm0, None, None, False, lambda e: None)
            for s in range(2):
                uses.n[s] += 1
                split_hi(act, s, 1)
            ffn_act(act, ffn, uses, 0, True)
            norm_act(act, norm1, ffn["y"], lambda t: 16 * (CHUNKS - 1) + 2 * t + 2, True,
                     lambda e: e.wait_ge(ffn["gu"], 8 * CHUNKS))
            for t in range(NT):
                act.wait_ge(mix["uv"], t + 1)
                if t == 0:
                    act.wait_ge(norm1["h"], NT)
                act.activation(u_sb[:, t, :], bank(t), ACT.Gelu_apprx_tanh).then_inc(mix["u"], 1)
                if t == 0:
                    nxt(0, mix["uv_half"], 1)
            nxt(1, mix["uv"], NT)
            act.wait_ge(mix["ws_turned"], 1)
            act.activation(ws_t[:, :, :], bank(7).rearrange("p (g t) -> p g t", g=G), ACT.Copy).then_inc(mix["ws"], 1)
            for t in range(NT):
                act.wait_ge(mix["uv"], NT + t + 1)
                if t >= 2:
                    act.wait_ge(mix["vn"], t - 1)
                act.activation(vg[:, t % 2, :], bank(t), ACT.Gelu_apprx_tanh).then_inc(mix["vg"], 1)
                if t == 0:
                    nxt(0, mix["uv_half"], 2)
            nxt(1, mix["uv"], 2 * NT)
            for t in range(NT):
                act.wait_ge(mix["v"], t + 1)
                if t == 0:
                    act.wait_ge(norm1["stored"], 16 * NT)
                act.activation(v_sb[:, t, :], bank(t), ACT.Copy).then_inc(mix["v_done"], 1)
                if t == 0:
                    nxt(0, mix["v_half"], 1)
            nxt(1, mix["v"], NT)
            for b in range(QK_BLOCKS):
                for n in range(4):
                    idx = 4 * b + n
                    act.wait_ge(mix["qk"], idx + 1)
                    if idx == 0:
                        act.wait_ge(mix["out_a"], G * NT)
                    tile, h = idx // 2, idx % 2
                    dst = (q_t if b < QK_BLOCKS // 2 else k_t)[:, tile % (SBW // P), h * HALF:(h + 1) * HALF]
                    act.activation(dst, bank(4 * (b % 2) + n), ACT.Copy,
                                   scale=HD ** -0.5 if b < QK_BLOCKS // 2 else 1.0).then_inc(mix["q"], 1)
                nxt(b % 2, mix["qk"], 4 * b + 4)

            for n in range(N_ATT + 2):
                if n < N_ATT:
                    i, h = att_step(n)
                    u, W = n % 2, (i + 1) * P
                    z = bank(2 * u, 2)[:, 0:W]
                    act.wait_ge(sb_att["z"], n + 1)
                    if n >= 2:
                        act.wait_ge(sb_att["turned"], n - 1)
                    act.activation(beta[:, u, 0:W], z, ACT.Sigmoid).then_inc(sb_att["beta"], 1)
                    act.activation(keep[:, u, 0:W], z, ACT.Sigmoid, scale=-1.0).then_inc(sb_att["keep"], 1)
                if n >= 2:
                    m = n - 2
                    i, h = att_step(m)
                    W = (i + 1) * P
                    act.wait_ge(sb_att["turned"], m + 1)
                    if m >= 2:
                        act.wait_ge(sb_att["av"], m - 1)
                    act.activation(attn_t[:, m % 2, 0:W], bank(4, 2)[:, 0:W], ACT.Copy).then_inc(sb_att["attn_t"], 1)
            nm = norm_merge
            for t in range(NT):
                if t:
                    act.wait_ge(nm["sum_h"], t)
                act.activation(square_out[:, 0:SW], u_sb[:, t, :], ACT.Square, accum_out=sums[:, t:t + 1]).then_inc(nm["sum_y"], 1)
                act.wait_ge(sb_att["out_b"], t + 1)
                act.wait_ge(nm["sum_y"], t + 1)
                act.activation(square_out[:, 0:SBW].rearrange("p (c d) -> p c d", d=P), out_b[:, :, t * P:(t + 1) * P],
                               ACT.Square, accum_out=sums[:, NT + t:NT + t + 1]).then_inc(nm["sum_h"], 1)
                if t >= 1:
                    turn_act(act, nm, t - 1, x_hi)
            turn_act(act, nm, NT - 1, x_hi)
            for cb in range(2):
                for t in range(NT):
                    act.wait_ge(wout["full"], cb * NT + t + 1)
                    act.activation(y[:, t, cb * BANK:(cb + 1) * BANK], bank(t), ACT.Copy).then_inc(wout["y"], 1)
                    if t == 0:
                        nxt(0, wout["half"], cb + 1)
                nxt(1, wout["full"], (cb + 1) * NT)
            norm_act(act, norm2, wout["y"], lambda t: NT + t + 1, True, lambda e: e.wait_ge(wout["full"], 2 * NT))
            norm_act(act, norm_mem, None, None, False, lambda e: e.wait_ge(norm2["h"], NT), None, NM)
            for b in range(XK_BLOCKS):
                for c in range(2):
                    act.wait_ge(xkv["k"], 2 * b + c + 1)
                    act.activation(mk_t[:, 2 * b + c, :], bank(4 * (b % 2) + 2 * c)[:, 0:M], ACT.Copy).then_inc(xkv["k_done"], 1)
                nxt(b % 2, xkv["k"], 2 * b + 2)
            for cb in range(2):
                for t in range(NM):
                    act.wait_ge(xkv["v"], cb * NM + t + 1)
                    act.activation(mv[:, t, cb * BANK:(cb + 1) * BANK], bank(t), ACT.Copy).then_inc(xkv["v_done"], 1)
                    if t == 0:
                        nxt(0, xkv["half"], cb + 1)
                nxt(1, xkv["v"], (cb + 1) * NM)
            for b in range(XK_BLOCKS):
                for n in range(4):
                    idx = 4 * b + n
                    act.wait_ge(xq["q"], idx + 1)
                    tile, h = idx // 2, idx % 2
                    act.activation(xq_t[:, tile, h * HALF:(h + 1) * HALF], bank(4 * (b % 2) + n), ACT.Copy).then_inc(xq["q_done"], 1)
                nxt(b % 2, xq["q"], 4 * b + 4)
            for t in range(NT):
                u = t % 2
                act.wait_ge(xatt["neg"], t + 1)
                if t >= 2:
                    act.wait_ge(xatt["turned"], t - 1)
                for h in range(XH_HEADS):
                    act.activation(probs[:, u, h, :], bank(2 * u, 2)[:, h * M:(h + 1) * M], ACT.Exp,
                                   bias=small[:, 48 + 4 * u + h:49 + 4 * u + h], scale=XHD ** -0.5,
                                   accum_out=small[:, 56 + 4 * u + h:57 + 4 * u + h]).then_inc(xatt["probs"], 1)
                if t >= 1:
                    o_hi_act(act, t - 1)
            o_hi_act(act, NT - 1)
            for cb in range(2):
                for t in range(NT):
                    act.wait_ge(xo["full"], cb * NT + t + 1)
                    act.activation(y[:, t, cb * BANK:(cb + 1) * BANK], bank(t), ACT.Copy).then_inc(xo["y"], 1)
                    if t == 0:
                        nxt(0, xo["half"], cb + 1)
                nxt(1, xo["full"], (cb + 1) * NT)
            norm_act(act, norm3, xo["y"], lambda t: NT + t + 1, True, lambda e: e.wait_ge(xo["full"], 2 * NT))
            act.wait_ge(norm3["stored"], 16 * NT)
            ffn_act(act, ffn, uses, CHUNKS, False)
            norm_act(act, norm4, ffn["y"], lambda t: 16 * (2 * CHUNKS - 1) + 2 * t + 2, True, None, stored_out)

        @block.vector
        def _(dve):
            uses = Uses()
            norm_dve(dve, norm0, 0.0, False)
            for s in range(2):
                next_lo(dve, uses, s)
            ffn_dve(dve, ffn, uses, 0, True)
            norm_dve(dve, norm1, 0.5, True)
            next_lo(dve, uses, 0)
            next_lo(dve, uses, 1)
            for t in range(NT):
                u = t % 2
                dve.wait_ge(mix["vg"], t + 1)
                st = small[:, 64 + 0:64 + 24].rearrange("p (g six) -> p g six", six=6)
                mv2 = small[:, 32 + 8 * u:40 + 8 * u].rearrange("p (g two) -> p g two", two=2)
                if t:
                    dve.wait_ge(mix["stats"], 4 * t)
                for g in range(G):
                    op = dve.bn_stats(st[:, g, :], vg[:, u, g * GD:(g + 1) * GD])
                    op.then_inc(mix["vn0"], 1)
                if t >= 2:
                    dve.wait_ge(mix["vn1"], 4 * (t - 1))
                for g in range(G):
                    dve.wait_ge(mix["vn0"], 4 * t + g + 1)
                    dve.bn_aggr(mv2[:, g, :], st[:, g, :]).then_inc(mix["stats"], 1)
                if t == 0:
                    dve.wait_ge(mix["const"], 64)
                dve.wait_ge(mix["rstd"], t + 1)
                if t >= 2:
                    dve.wait_ge(mix["gated"], t - 1)
                for g in range(G):
                    dve.tensor_scalar(vn[:, u, g * GD:(g + 1) * GD], vg[:, u, g * GD:(g + 1) * GD], mv2[:, g, 0:1],
                                      mv2[:, g, 1:2], ALU.subtract, ALU.mult).then_inc(mix["vn1"], 1)
                dve.wait_ge(mix["vn1"], 4 * t + 4)
                dve.tensor_tensor(vn[:, u, :], vn[:, u, :], sgu_bc[:, 0, :], ALU.mult).then_inc(mix["vn1b"], 1)
                dve.wait_ge(mix["vn1b"], t + 1)
                dve.tensor_tensor(vn[:, u, :], vn[:, u, :], sgu_bc[:, 1, :], ALU.add).then_inc(mix["vn"], 1)
                if t >= 1:
                    gate_dve(dve, t - 1)
                if t == 1:
                    next_lo(dve, uses, 0)
            gate_dve(dve, NT - 1)
            next_lo(dve, uses, 1)
            next_lo(dve, uses, 0)
            next_lo(dve, uses, 1)
            for b in range(QK_BLOCKS):
                next_lo(dve, uses, b % 2)
            dve.memset(suffix[:, :, :], 1.0).then_inc(sb_att["ones"], 1)
            dve.wait_ge(sb_att["ones"], 1)
            for n in range(N_ATT):
                i, h = att_step(n)
                u, W = n % 2, (i + 1) * P
                dve.wait_ge(sb_att["keep"], n + 1)
                if n >= 2:
                    dve.wait_ge(sb_att["attn"], n - 1)
                dve.tensor_tensor_scan(suffix[:, u, 0:W][:, ::-1], keep[:, u, 0:W][:, ::-1], keep[:, u, 0:W][:, ::-1],
                                       1.0, ALU.mult, ALU.bypass).then_inc(sb_att["suffix"], 1)
                dve.wait_ge(sb_att["suffix"], n + 1)
                dve.tensor_tensor(beta[:, u, 0:W], beta[:, u, 0:W], suffix[:, u, 1:W + 1], ALU.mult).then_inc(sb_att["attn"], 1)
                if n >= SBH + 2 and (n - 2) % SBH == 0:
                    out_b_dve(dve, (n - 2) // SBH - 1)
            out_b_dve(dve, NT - 1)
            nm = norm_merge
            for t in range(NT):
                u = t % 2
                if t == 0:
                    dve.wait_ge(nm["gain_pre"], 32)
                if t >= 2:
                    dve.wait_ge(nm["turned"], t - 1)
                dve.wait_ge(nm["rstd_y"], t + 1)
                dve.scalar_tensor_tensor(normed[:, u, 0:SW], u_sb[:, t, :], rstd[:, t:t + 1], gain_pre[:, 0:SW],
                                         ALU.mult, ALU.mult)
                dve.wait_ge(nm["rstd_h"], t + 1)
                dve.scalar_tensor_tensor(normed[:, u, SW:D].rearrange("p (c d) -> p c d", d=P), out_b[:, :, t * P:(t + 1) * P],
                                         rstd[:, NT + t:NT + t + 1], gain_pre[:, SW:D].rearrange("p (c d) -> p c d", d=P),
                                         ALU.mult, ALU.mult).then_inc(nm["normed"], 1)
                if t >= 1:
                    turn_dve(dve, nm, t - 1, x_hi, x_lo)
            turn_dve(dve, nm, NT - 1, x_hi, x_lo)
            for s in (0, 1, 0, 1):
                next_lo(dve, uses, s)
            norm_dve(dve, norm2, 1.0, True)
            norm_dve(dve, norm_mem, 0.0, False, None, NM)
            for _ in range(XK_BLOCKS // 2 + 2 + XK_BLOCKS // 2):
                next_lo(dve, uses, 0)
                next_lo(dve, uses, 1)
            for t in range(NT):
                u = t % 2
                dve.wait_ge(xatt["logits"], t + 1)
                if t >= 2:
                    dve.wait_ge(xatt["probs"], 4 * (t - 1))
                dve.tensor_reduce(small[:, 32 + 4 * u:36 + 4 * u], bank(2 * u, 2).rearrange("p (h m) -> p h m", m=M),
                                  AX.X, ALU.max).then_inc(xatt["max"], 1)
                dve.wait_ge(xatt["max"], t + 1)
                dve.tensor_scalar(small[:, 48 + 4 * u:52 + 4 * u], small[:, 32 + 4 * u:36 + 4 * u], -(XHD ** -0.5), None,
                                  ALU.mult).then_inc(xatt["neg"], 1)
                dve.wait_ge(xatt["probs"], 4 * t + 4)
                if t >= 2:
                    dve.wait_ge(xatt["scaled"], 4 * (t - 1))
                dve.reciprocal(small[:, 40 + 4 * u:44 + 4 * u], small[:, 56 + 4 * u:60 + 4 * u]).then_inc(xatt["recip"], 1)
                dve.wait_ge(xatt["recip"], t + 1)
                for h in range(XH_HEADS):
                    dve.tensor_scalar(probs[:, u, h, :], probs[:, u, h, :], small[:, 40 + 4 * u + h:41 + 4 * u + h], None,
                                      ALU.mult).then_inc(xatt["scaled"], 1)
                if t >= 1:
                    o_lo_dve(dve, t - 1)
                dve.wait_ge(xatt["turned"], t + 1)
                dve.tensor_copy(probs_t[:, :], bank(4, 2)).then_inc(xatt["probs_t"], 1)
            o_lo_dve(dve, NT - 1)
            for s in (0, 1, 0, 1):
                next_lo(dve, uses, s)
            norm_dve(dve, norm3, 1.0, True)
            ffn_dve(dve, ffn, uses, CHUNKS, False)
            norm_dve(dve, norm4, 0.5, True, stored_out)

        @block.tensor
        def _(pe):
            uses = Uses()
            pe.wait_ge(const["made"], 2)
            norm_pe(pe, norm0, NT, lambda: None)

            ffn_pe(pe, ffn, uses, 0, norm0["x_full"])
            norm_pe(pe, norm1, NT, lambda: pe.wait_ge(ffn["y"], 16 * CHUNKS))
            pe.wait_ge(norm1["x_full"], NT)
            project_rows_pe(pe, uses, mix["uv_half"], mix["uv"], 0, NT, x_hi, x_lo, lambda t: None)
            pe.wait_ge(mix["masked"], 1)
            pe.wait_ge(mix["u"], NT)
            for g in range(G):
                mm = pe.transpose(bank(7)[:, g * P:(g + 1) * P], ws_raw[:, g, :], ident[:, :])
            mm.then_inc(mix["ws_turned"], 1)
            project_rows_pe(pe, uses, mix["uv_half"], mix["uv"], 1, NT, x_hi, x_lo,
                            lambda t: pe.wait_ge(mix["ws"], 1) if t == 7 else None)
            for t in range(NT):
                pe.wait_ge(mix["vn"], t + 1)
                for g in range(G):
                    at = slice(g * GD, (g + 1) * GD)
                    mm = pe.matmul(bank(t)[:, at], ws_t[:, g, :], vn[:, t % 2, at], start=True, stop=True)
                mm.then_inc(mix["gated"], 1)
            project_rows_pe(pe, uses, mix["v_half"], mix["v"], 0, NT, x_hi, x_lo, lambda t: pe.wait_ge(mix["out_a"], G * (t + 1)))
            for b in range(QK_BLOCKS):
                def free(bk):
                    if b < 2:
                        pe.wait_ge(mix["v_done"], bk + 1)
                    else:
                        pe.wait_ge(mix["q"], 4 * (b - 2) + bk % 4 + 1)
                project_cols_pe(pe, uses, mix["qk"], b % 2, S, x_hi, x_lo, free)
            pe.wait_ge(mix["q"], 4 * QK_BLOCKS)

            def scores(n):
                i, h = att_step(n)
                u, W = n % 2, (i + 1) * P
                if n >= 2:
                    pe.wait_ge(sb_att["keep"], n - 1)
                rows = slice(HD * (h % 2), HD * (h % 2) + HD)
                z = bank(2 * u, 2)
                for c0 in range(0, W, BANK):
                    c1 = min(W, c0 + BANK)
                    last = c1 == W
                    mm = pe.matmul(z[:, c0:c1], q_t[rows, h // 2, i * P:(i + 1) * P], k_t[rows, h // 2, c0:c1],
                                   start=True, stop=not last)
                    if last:
                        mm = pe.matmul(z[:, W - P:W], ident[:, :], causal_neg[:, :], start=False, stop=True)
                mm.then_inc(sb_att["z"], 1)

            def turns(n):
                i, h = att_step(n)
                pe.wait_ge(sb_att["attn"], n + 1)
                if n >= 1:
                    pe.wait_ge(sb_att["attn_t"], n)
                for j in range(i + 1):
                    mm = pe.transpose(bank(4, 2)[:, j * P:(j + 1) * P], beta[:, n % 2, j * P:(j + 1) * P], ident[:, :])
                mm.then_inc(sb_att["turned"], 1)

            def values(n):
                i, h = att_step(n)
                pe.wait_ge(sb_att["attn_t"], n + 1)
                if h == 0 and i >= 2:
                    pe.wait_ge(sb_att["out_b"], i - 1)
                for j in range(i + 1):
                    mm = pe.matmul(bank(6 + i % 2)[:, h * HD:(h + 1) * HD], attn_t[:, n % 2, j * P:(j + 1) * P],
                                   v_sb[:, j, h * HD:(h + 1) * HD], start=j == 0, stop=j == i)
                mm.then_inc(sb_att["av"], 1)

            scores(0)
            for n in range(N_ATT + 2):
                if n + 1 < N_ATT:
                    scores(n + 1)
                if n >= 1 and n - 1 < N_ATT:
                    turns(n - 1)
                if n >= 2:
                    values(n - 2)
            norm_pe(pe, norm_merge, NT, lambda: pe.wait_ge(sb_att["out_b"], NT))
            pe.wait_ge(norm_merge["x_full"], NT)
            for cb in range(2):
                project_rows_pe(pe, uses, wout["half"], wout["full"], cb, NT, x_hi, x_lo,
                                lambda t: pe.wait_ge(wout["y"], (cb - 1) * NT + t + 1) if cb else None)
            norm_pe(pe, norm2, NT, lambda: pe.wait_ge(wout["y"], 2 * NT))
            norm_pe(pe, norm_mem, NM, lambda: pe.wait_ge(norm2["x_full"], NT))
            pe.wait_ge(norm_mem["x_full"], NM)
            for b in range(XK_BLOCKS):
                project_cols_pe(pe, uses, xkv["k"], b % 2, M, m_hi, m_lo,
                                lambda bk: pe.wait_ge(xkv["k_done"], 2 * (b - 2) + (bk % 4) // 2 + 1) if b >= 2 else None)
            pe.wait_ge(xkv["k_done"], 2 * XK_BLOCKS)
            for cb in range(2):
                project_rows_pe(pe, uses, xkv["half"], xkv["v"], cb, NM, m_hi, m_lo,
                                lambda t: pe.wait_ge(xkv["v_done"], (cb - 1) * NM + t + 1) if cb else None)
            pe.wait_ge(xkv["v_done"], 2 * NM)
            for b in range(XK_BLOCKS):
                project_cols_pe(pe, uses, xq["q"], b % 2, S, x_hi, x_lo,
                                lambda bk: pe.wait_ge(xq["q_done"], 4 * (b - 2) + bk % 4 + 1) if b >= 2 else None)
            pe.wait_ge(xq["q_done"], 4 * XK_BLOCKS)

            def logits(t):
                if t >= 2:
                    pe.wait_ge(xatt["probs"], 4 * (t - 1))
                for h in range(XH_HEADS):
                    for c in range(2):
                        mm = pe.matmul(bank(2 * (t % 2), 2)[:, h * M:(h + 1) * M], xq_t[:, 2 * h + c, t * P:(t + 1) * P],
                                       mk_t[:, 2 * h + c, :], start=c == 0, stop=c == 1)
                mm.then_inc(xatt["logits"], 1)

            def turn_probs(t):
                pe.wait_ge(xatt["scaled"], 4 * t + 4)
                if t >= 1:
                    pe.wait_ge(xatt["probs_t"], t)
                for h in range(XH_HEADS):
                    for m in range(NM):
                        mm = pe.transpose(bank(4, 2)[:, (h * NM + m) * P:(h * NM + m + 1) * P],
                                          probs[:, t % 2, h, m * P:(m + 1) * P], ident[:, :])
                mm.then_inc(xatt["turned"], 1)

            def mem_values(t):
                pe.wait_ge(xatt["probs_t"], t + 1)
                if t >= 1:
                    pe.wait_ge(xatt["o_full"], t)
                for k in range(NK):
                    h = k // (NK // XH_HEADS)
                    for m in range(NM):
                        mm = pe.matmul(bank(6, 2)[:, k * P:(k + 1) * P], mv[:, m, k * P:(k + 1) * P],
                                       probs_t[:, (h * NM + m) * P:(h * NM + m + 1) * P], start=m == 0, stop=m == NM - 1)
                mm.then_inc(xatt["o"], 1)

            logits(0)
            for t in range(NT):
                if t + 1 < NT:
                    logits(t + 1)
                turn_probs(t)
                mem_values(t)
            pe.wait_ge(xatt["o_full"], NT)
            for cb in range(2):
                project_rows_pe(pe, uses, xo["half"], xo["full"], cb, NT, x_hi, x_lo,
                                lambda t: pe.wait_ge(xo["y"], (cb - 1) * NT + t + 1) if cb else None)
            norm_pe(pe, norm3, NT, lambda: pe.wait_ge(xo["y"], 2 * NT))
            ffn_pe(pe, ffn, uses, CHUNKS, norm3["x_full"])


_INS = ["x", "mem", "ffn1_pre_g", "ffn1_post_g", "ffn1_w_gate", "ffn1_w_up", "ffn1_w_down", "mix_pre_g",
        "mix_post_g", "w_in", "sgu_norm_g", "sgu_norm_b", "sgu_w_s", "sgu_b_s", "sgu_out_g", "sb_out_g", "w_out",
        "xa_pre_g", "xa_post_g", "mem_norm_g", "xa_w_q", "xa_w_kv", "xa_w_o", "ffn2_pre_g", "ffn2_post_g",
        "ffn2_w_gate", "ffn2_w_up", "ffn2_w_down", "final_norm_g"]


def kernel(**inputs):
    import numpy as _np
    import concourse.bacc as _bacc
    from concourse import mybir as _mybir
    from concourse.bass_utils import run_bass_kernel_spmd as _run

    nc = _bacc.Bacc("TRN2", target_bir_lowering=False, num_devices=1)
    arrays, args = {}, {}
    for name in _INS:
        v = _np.ascontiguousarray(inputs[name])
        arrays[f"in_{name}"] = v
        args[name] = nc.dram_tensor(f"in_{name}", v.shape, _mybir.dt.from_np(v.dtype), kind="ExternalInput").ap()
    out = nc.dram_tensor("out_0", inputs["x"].shape, _mybir.dt.float32, kind="ExternalOutput").ap()
    build(nc, args, out)
    r = _run(nc, [arrays], core_ids=[0])
    return r.results[0]["out_0"]
```

```python
from contextlib import ExitStack

import concourse.bass as bass
from concourse import mybir

ACT = mybir.ActivationFunctionType
ALU = mybir.AluOpType
AX = mybir.AxisListType
F32 = mybir.dt.float32
F32R = mybir.dt.float32r
BF16 = mybir.dt.bfloat16

P = 128
BANK = 512
EPS = 1e-6
MASKED = -1e30


class Uses:

    def __init__(self):
        self.n = [0, 0, 0]


def build(nc, a, out):
    S, D = a["x"].shape[1:]
    M = a["mem"].shape[1]
    FF = a["ffn1_w_gate"].shape[2]
    G, CH = a["sgu_w_s"].shape[1:3]
    SW = a["sgu_out_g"].shape[1]
    GD = SW // G
    SBW = a["sb_out_g"].shape[1]
    HD = 64
    SBH = SBW // HD
    XHEADS = 4
    XHD = D // XHEADS
    NT = S // P
    NK = D // P
    NM = M // P
    NF = FF // P
    CHUNKS = NF // 2
    PAIRS = NT // 2
    SLOT = 2 * D
    HALF = S // 2
    COLS = 256
    QK_BLOCKS = 2 * SBW // COLS
    XK_BLOCKS = D // COLS
    N_ATT = NT * SBH
    U_COLS, VG_COLS, Q_COLS = 0, SW, 2 * SW
    V_COLS = 2 * SW + 2 * SBW
    assert S == D == 1024 and NF % 2 == 0 and CH == P and GD == P and HALF == BANK == SW == SBW and NM == 2

    ctx = ExitStack()
    with ctx:
        def sem(name):
            return ctx.enter_context(nc.semaphore(name))

        def sems(stage, *names):
            return {n: sem(f"{stage}_{n}") for n in names}

        def sb(name, shape, dt=F32):
            return ctx.enter_context(nc.sbuf_tensor(name, shape, dt))

        def overlay(*tensors):
            with ExitStack() as place:
                return [place.enter_context(nc.sbuf_tensor(n, shape, dt)) for n, shape, dt in tensors]

        w_raw = sb("w_raw", [P, 2, SLOT])
        w_hi = sb("w_hi", [P, 2, SLOT], F32R)
        w_lo = sb("w_lo", [P, 2, SLOT], F32R)
        resid_a, vg = overlay(("resid_a", [P, 2, D], F32), ("vg", [P, NT, SW], F32))
        mem_v, = overlay(("mem_v", [P, NM, D], F32))
        q_odd, = overlay(("q_odd", [P, SBW // P, S], F32))
        w2_raw = sb("w2_raw", [P, SLOT])
        w2_hi = sb("w2_hi", [P, SLOT], F32R)
        w2_lo = sb("w2_lo", [P, SLOT], F32R)
        m_hi = w2_hi[:, :].rearrange("p (k m) -> p k m", m=M)
        m_lo = w2_lo[:, :].rearrange("p (k m) -> p k m", m=M)

        ident = sb("ident", [P, P])
        ident_bf = sb("ident_bf", [P, P], BF16)
        causal_neg = sb("causal_neg", [P, P], BF16)
        ws_t, = overlay(("ws_t", [P, G, P], F32))
        square_out = sb("square_out", [P, D], BF16)
        sgu_bc = sb("sgu_bc", [P, 2, SW])
        sums = sb("sums", [P, 2 * NT])
        rstd = sb("rstd", [P, 2 * NT])
        half_pow = sb("half_pow", [P, 8])
        small = sb("small", [P, 96])

        beta, keep, suffix, attn_t = overlay(
            ("beta", [P, 2, S], F32), ("keep", [P, 2, S], F32), ("suffix", [P, 2, S + 8], F32),
            ("attn_t", [P, 2, S], F32))
        x_hi = sb("x_hi", [P, NK, S], F32R)
        x_lo = sb("x_lo", [P, NK, S], F32R)

        u_sb, q_even, v_sb, k_t = overlay(
            ("u_sb", [P, NT, SW], F32), ("q_even", [P, SBW // P, S], F32), ("v_sb", [P, NT, SBW], F32),
            ("k_t", [P, SBW // P, S], F32))
        out_b = q_even
        xq_t, resid_b, mem_k, probs, probs_t = overlay(
            ("xq_t", [P, NK, S], F32), ("resid_b", [P, 2, D], F32), ("mem_k", [P, NK, M], F32),
            ("probs", [P, 2, XHEADS, M], F32), ("probs_t", [P, D], F32))
        y = sb("y", [P, NT, D])
        ws_raw, = overlay(("ws_raw", [P, G, P], F32))
        hid_hi = sb("hid_hi", [P, 2, S], F32R)
        hid_lo = sb("hid_lo", [P, 2, S], F32R)
        normed, = overlay(("normed", [P, 2, D], F32))
        gate_act = sb("gate_act", [P, 2, HALF])
        product = sb("product", [P, 2, HALF])
        gain_post = sb("gain_post", [P, D])
        gain_pre = sb("gain_pre", [P, D])

        def raw(s):
            return w_raw[:, s, :] if s < 2 else w2_raw[:, :]

        def hi(s):
            return w_hi[:, s, :] if s < 2 else w2_hi[:, :]

        def lo(s):
            return w_lo[:, s, :] if s < 2 else w2_lo[:, :]

        ps = ctx.enter_context(nc.psum_tensor("ps", [P, 8, BANK], F32))

        def bank(b, n=1):
            return ps[:, b:b + n, :].rearrange("p b c -> p (b c)")

        def turn_bank(t):
            return bank(4 + 2 * (t % 2), 2)

        h_dram = [nc.dram_tensor(f"h_scratch{i}", [S, D], F32, kind="Internal").ap() for i in range(3)]
        x_in = a["x"][0]

        raw_full = [sem(f"raw_full{s}") for s in range(3)]
        hi_done = [sem(f"hi_done{s}") for s in range(3)]
        w_full = [sem(f"w_full{s}") for s in range(3)]
        const = sems("const", "zero", "made")
        mean_square = sem("mean_square")

        PRE = ("gains", "sum_h", "rstd_h", "normed")
        POST = ("sum_y", "rstd_y", "scaled", "h", "stored0", "stored1")
        TURN = ("turned", "x_hi", "x_full")
        norm0 = sems("norm0", *PRE, *TURN)
        norm1 = sems("norm1", *POST, *PRE, *TURN)
        merge = sems("merge", *PRE, *TURN, "sum_y", "rstd_y", "left")
        norm2 = sems("norm2", *POST, *PRE, *TURN)
        norm3 = sems("norm3", *POST, *PRE, *TURN)
        norm4 = sems("norm4", "gains", "sum_y", "rstd_y", "scaled", "h", "sum_h", "rstd_h", "unit", "normed")
        norm_mem = sems("norm_mem", *PRE, *TURN)
        x_tile = [sem(f"x_tile{t}") for t in range(NT)]
        resid_full = [sem(f"resid_full{u}") for u in range(2)]
        norm1["loads"], norm_mem["loads"], norm2["loads"] = 0, NT // 2, (NT + NM) // 2
        norm3["loads"], norm4["loads"] = (2 * NT + NM) // 2, (3 * NT + NM) // 2

        ffn = sems("ffn", "gu", "gate_act", "product", "hid_hi", "hid_full", "down", "y")
        mix = sems("mix", "half", "full", "u", "vg", "bn", "stats", "rstd", "centred", "gained", "vn", "mixed",
                   "out_a", "qk", "qk_done", "const", "ws_raw", "masked", "ws_turned", "ws", "v_done", "padded")
        sb_att = sems("sb", "ones", "z", "beta", "keep", "suffix", "attn", "turned", "attn_t", "av", "out_b")
        wout = sems("wout", "half", "full", "y")
        xkv = sems("xkv", "k", "k_done", "half", "v", "v_done")
        xq = sems("xq", "q", "q_done")
        xatt = sems("xatt", "logits", "max", "neg", "probs", "recip", "scaled", "turned", "probs_t", "o", "o_hi",
                    "o_full")
        xo = sems("xo", "half", "full", "y")
        stored_out = sem("stored_out")

        block = ctx.enter_context(nc.Block())

        def load_block(sp, uses, s, halves, ahead=0):
            n = uses.n[s]
            if n or not isinstance(ahead, int):
                sp.wait_ge(w_full[s], n + ahead)
            for dst, src in halves:
                sp.dma_start(dst, src).then_inc(raw_full[s], 16)

        def block_cols(name, s, c0):
            w = a[name][0].rearrange("(k p) c -> p k c", p=P)
            dst = raw(s).rearrange("p (k c) -> p k c", c=COLS)
            h = NK // 2
            return [(dst[:, i * h:(i + 1) * h, :], w[:, i * h:(i + 1) * h, c0:c0 + COLS]) for i in range(2)]

        def block_rows(name, s, k0, c0):
            w = a[name][0].rearrange("(k p) c -> p k c", p=P)
            dst = raw(s).rearrange("p (k c) -> p k c", c=BANK)
            return [(dst[:, 2 * i:2 * i + 2, :], w[:, k0 + 2 * i:k0 + 2 * i + 2, c0:c0 + BANK]) for i in range(2)]

        def gate_up(p, f, tile):
            dst = raw(f).rearrange("p (g k c) -> p g k c", g=2, c=P)
            gate = a[p + "_w_gate"][0].rearrange("(k p) c -> p k c", p=P)
            up = a[p + "_w_up"][0].rearrange("(k p) c -> p k c", p=P)
            return [(dst[:, 0], gate[:, :, bass.ds(tile * P, P)]), (dst[:, 1], up[:, :, bass.ds(tile * P, P)])]

        def down_rows(p, chunk):
            w = a[p + "_w_down"][0].rearrange("(f p) c -> p f c", p=P)
            return [(w2_raw[:, f * D:(f + 1) * D], w[:, bass.ds(2 * chunk + f, 1), :].rearrange("p f c -> p (f c)"))
                    for f in range(2)]

        @block.sync
        def _(sp):
            uses = Uses()

            def one(s, halves):
                load_block(sp, uses, s, halves)
                uses.n[s] += 1

            def rows(name, c0):
                for s in range(2):
                    one(s, block_rows(name, s, 4 * s, c0))

            def ffn_rest(p):
                one(2, down_rows(p, 0))
                with sp.Fori(1, CHUNKS) as i:
                    for f in range(2):
                        load_block(sp, uses, f, gate_up(p, f, 2 * i + f), i - 1)
                    load_block(sp, uses, 2, down_rows(p, i), i - 1)
                for s in range(3):
                    uses.n[s] += CHUNKS - 1

            def x_tiles(t0, t1):
                for t in range(t0, t1):
                    sp.dma_start(y[:, t, :], x_in[t * P:(t + 1) * P, :]).then_inc(x_tile[t], 16)

            x_tiles(0, 2)
            sp.dma_start(gain_pre[:, :], a["ffn1_pre_g"].broadcast_to((P, D))).then_inc(norm0["gains"], 16)
            x_tiles(2, 3)
            one(0, gate_up("ffn1", 0, 0))
            x_tiles(3, 6)
            one(1, gate_up("ffn1", 1, 1))
            x_tiles(6, NT)
            ffn_rest("ffn1")
            rows("w_in", U_COLS)
            sp.dma_start(sgu_bc[:, 0, :], a["sgu_norm_g"][0].rearrange("(o g) d -> o (g d)", o=1)
                         .broadcast_to((P, SW))).then_inc(mix["const"], 16)
            sp.dma_start(sgu_bc[:, 1, :], a["sgu_norm_b"][0].rearrange("(o g) d -> o (g d)", o=1)
                         .broadcast_to((P, SW))).then_inc(mix["const"], 16)
            sp.dma_start(small[:, 0:G], a["sgu_b_s"][0].rearrange("g t -> t g"),
                         allow_slow_non_contiguous=True).then_inc(mix["const"], 16)
            sp.wait_ge(ffn["down"], 2 * NT * CHUNKS)
            sp.dma_start(ws_raw[:, :, :], a["sgu_w_s"][0].rearrange("g t s -> t g s")).then_inc(mix["ws_raw"], 16)
            rows("w_in", VG_COLS)
            rows("w_in", V_COLS)
            for b in range(QK_BLOCKS):
                one(b % 2, block_cols("w_in", b % 2, Q_COLS + b * COLS))
            for cb in range(2):
                rows("w_out", cb * BANK)
            for b in range(XK_BLOCKS):
                one(b % 2, block_cols("xa_w_kv", b % 2, b * COLS))
            for cb in range(2):
                rows("xa_w_kv", D + cb * BANK)
            for b in range(XK_BLOCKS):
                one(b % 2, block_cols("xa_w_q", b % 2, b * COLS))
            for cb in range(2):
                rows("xa_w_o", cb * BANK)
            for f in range(2):
                one(f, gate_up("ffn2", f, f))
            sp.wait_ge(xatt["o"], NT)
            ffn_rest("ffn2")
            for t in range(NT):
                sp.wait_ge(norm4["normed"], t + 1)
                sp.dma_start(out[0, t * P:(t + 1) * P, :], y[:, t, :]).then_inc(stored_out, 16)
            sp.wait_ge(stored_out, 16 * NT)

        squares = [0]

        def after(pool, op):
            squares[0] += 1
            op.then_inc(mean_square, 1)
            pool.wait_ge(mean_square, squares[0])

        def rstd_y(pool, s, t, width=D):
            pool.wait_ge(s["sum_y"], t + 1)
            after(pool, pool.tensor_scalar(sums[:, t:t + 1], sums[:, t:t + 1], 1.0 / width, EPS, ALU.mult, ALU.add))
            pool.tensor_tensor(rstd[:, t:t + 1], sums[:, t:t + 1], half_pow[:, 0:1], ALU.pow).then_inc(s["rstd_y"], 1)

        def rstd_h(pool, s, t, width=D):
            col = slice(NT + t, NT + t + 1)
            pool.wait_ge(s["sum_h"], t + 1)
            after(pool, pool.tensor_scalar(sums[:, col], sums[:, col], 1.0 / width, EPS, ALU.mult, ALU.add))
            pool.tensor_tensor(rstd[:, col], sums[:, col], half_pow[:, 0:1], ALU.pow).then_inc(s["rstd_h"], 1)

        @block.gpsimd
        def _(pool):
            pool.memset(half_pow[:, :], -0.5).then_inc(const["zero"], 1)
            pool.memset(ident[:, :], 0.0).then_inc(const["zero"], 1)
            pool.memset(ident_bf[:, :], 0.0).then_inc(const["zero"], 1)
            pool.memset(causal_neg[:, :], 0.0).then_inc(const["zero"], 1)
            pool.wait_ge(const["zero"], 4)
            for m in (ident, ident_bf):
                pool.affine_select(out=m[:, :], in_=m[:, :], compare_op=ALU.not_equal, fill=1.0, base=0,
                                   pattern=[[-1, P]], channel_multiplier=1).then_inc(const["made"], 1)
            pool.affine_select(out=causal_neg[:, :], in_=causal_neg[:, :], compare_op=ALU.is_gt, fill=MASKED,
                               base=0, pattern=[[-1, P]], channel_multiplier=1).then_inc(const["made"], 1)
            for t in range(NT):
                rstd_h(pool, norm0, t)

            def norm_pairs(s):
                for p in range(PAIRS):
                    for t in (2 * p, 2 * p + 1):
                        rstd_y(pool, s, t)
                    for t in (2 * p, 2 * p + 1):
                        rstd_h(pool, s, t)

            norm_pairs(norm1)
            pool.wait_ge(mix["ws_raw"], 16)
            pool.affine_select(out=ws_raw[:, :, :], in_=ws_raw[:, :, :], compare_op=ALU.is_ge, fill=0.0, base=0,
                               pattern=[[0, G], [-1, P]], channel_multiplier=1).then_inc(mix["masked"], 1)
            for t in range(NT):
                pool.wait_ge(mix["stats"], G * (t + 1))
                var = small[:, 32 + 8 * (t % 2):40 + 8 * (t % 2)].rearrange("p (g two) -> p g two", two=2)[:, :, 1]
                after(pool, pool.tensor_scalar(var, var, 1.0, EPS, ALU.mult, ALU.add))
                pool.tensor_tensor(var, var, half_pow[:, 0:G], ALU.pow).then_inc(mix["rstd"], 1)
            pool.wait_ge(norm1["stored1"], 16 * PAIRS)
            pool.wait_ge(norm1["normed"], NT)
            pool.wait_ge(mix["rstd"], NT)
            pool.memset(q_even[HD:P, :, :], 0.0).then_inc(mix["padded"], 1)
            pool.wait_ge(mix["mixed"], NT)
            pool.wait_ge(mix["padded"], 1)
            pool.memset(q_odd[0:HD, :, :], 0.0).then_inc(mix["padded"], 1)
            pool.wait_ge(mix["padded"], 2)
            for t in range(NT):
                rstd_y(pool, merge, t, SW)
                rstd_h(pool, merge, t, SBW)
            for t in range(NM):
                rstd_h(pool, norm_mem, t)
            norm_pairs(norm2)
            norm_pairs(norm3)
            for p in range(PAIRS):
                for t in (2 * p, 2 * p + 1):
                    rstd_y(pool, norm4, t)
                for t in (2 * p, 2 * p + 1):
                    rstd_h(pool, norm4, t)
                for t in (2 * p, 2 * p + 1):
                    pool.wait_ge(norm4["unit"], t + 1)
                    pool.tensor_tensor(y[:, t, :], y[:, t, :], gain_pre[:, :], ALU.mult).then_inc(norm4["normed"], 1)

        def split_hi(act, s, n):
            act.wait_ge(raw_full[s], n * 32)
            act.activation(hi(s), raw(s), ACT.Copy).then_inc(hi_done[s], 1)

        def next_hi(act, uses, s, ready, n):
            act.wait_ge(ready, n)
            uses.n[s] += 1
            split_hi(act, s, uses.n[s])

        def load_resid(act, s, place, src, t):
            act.dma_start(place[:, t % 2, :], src[t * P:(t + 1) * P, :]).then_inc(resid_full[t % 2], 16)

        def wait_resid(eng, s, t):
            eng.wait_ge(resid_full[t % 2], 16 * (s["loads"] + t // 2 + 1))

        def load_gains(act, s, post, pre):
            if post is not None:
                act.dma_start(gain_post[:, :], a[post].broadcast_to((P, D))).then_inc(s["gains"], 16)
            act.dma_start(gain_pre[:, :], a[pre].broadcast_to((P, D))).then_inc(s["gains"], 16)

        def ffn_act(act, uses, c0, prefetch_last):
            def hidden(i, q, first):
                f, h = q % 2, q // 2
                idx = 4 * i + q
                act.wait_ge(ffn["gu"], 2 * idx + 1)
                if not (first and q < 2):
                    act.wait_ge(ffn["product"], idx - 1)
                act.activation(gate_act[:, q % 2, :], bank(2 * (q % 2)), ACT.Silu).then_inc(ffn["gate_act"], 1)
                act.wait_ge(ffn["product"], idx + 1)
                if not first:
                    act.wait_ge(ffn["down"], 2 * NT * i)
                act.activation(hid_hi[:, f, h * HALF:(h + 1) * HALF], product[:, q % 2, :], ACT.Copy)\
                   .then_inc(ffn["hid_hi"], 1)

            def chunk(i, first, last):
                hidden(i, 0, first)
                if not first:
                    act.wait_ge(ffn["down"], 2 * NT * i)
                split_hi(act, 2, uses.n[2] + 1 - c0 + i)
                hidden(i, 1, first)
                hidden(i, 2, first)
                if prefetch_last or not last:
                    act.wait_ge(ffn["gu"], 8 * i + 6)
                    split_hi(act, 0, uses.n[0] + 1 - c0 + i)
                hidden(i, 3, first)
                if prefetch_last or not last:
                    act.wait_ge(ffn["gu"], 8 * i + 8)
                    split_hi(act, 1, uses.n[1] + 1 - c0 + i)

            chunk(c0, True, False)
            with act.Fori(c0 + 1, c0 + CHUNKS - 1) as i:
                chunk(i, False, False)
            chunk(c0 + CHUNKS - 1, False, True)
            uses.n[2] += CHUNKS
            for f in range(2):
                uses.n[f] += CHUNKS - (not prefetch_last)

        @block.scalar
        def _(act):
            uses = Uses()
            last_square = []

            def square_sum(src, col, done, n, width=D, parts=None):
                if last_square:
                    act.wait_ge(*last_square[-1])
                dst = square_out[:, 0:width]
                if parts:
                    dst = dst.rearrange("p (c d) -> p c d", d=parts)
                act.activation(dst, src, ACT.Square, accum_out=sums[:, col:col + 1]).then_inc(done, 1)
                last_square.append((done, n))

            def square_y(s, t):
                square_sum(y[:, t, :], t, s["sum_y"], t + 1)

            def square_h(s, t, store, place, src):
                act.wait_ge(s["h"], t + 1)
                square_sum(y[:, t, :], NT + t, s["sum_h"], t + 1)
                if store is not None:
                    act.dma_start(store[t * P:(t + 1) * P, :], y[:, t, :]).then_inc(s[f"stored{t // PAIRS}"], 16)
                if t + 2 < NT:
                    load_resid(act, s, place, src, t + 2)

            def turn_hi(s, t, dst):
                act.wait_ge(s["turned"], t + 1)
                act.activation(dst[:, :, t * P:(t + 1) * P], turn_bank(t).rearrange("p (k c) -> p k c", c=P),
                               ACT.Copy).then_inc(s["x_hi"], 1)

            def norm_pair(s, p, projected, store, place, src):
                pair = (2 * p, 2 * p + 1)
                for t in pair:
                    act.wait_ge(projected, NT + t + 1)
                    square_y(s, t)
                for t in pair:
                    square_h(s, t, store, place, src)
                for t in pair:
                    turn_hi(s, t, x_hi)

            def project_y(s, cb, t):
                act.wait_ge(s["full"], cb * NT + t + 1)
                act.activation(y[:, t, cb * BANK:(cb + 1) * BANK], bank(t % 4), ACT.Copy).then_inc(s["y"], 1)

            for t in range(NT):
                act.wait_ge(x_tile[t], 16)
                square_sum(y[:, t, :], NT + t, norm0["sum_h"], t + 1)
                if t == 2:
                    uses.n[0] += 1
                    split_hi(act, 0, 1)
                if t == 4:
                    uses.n[1] += 1
                    split_hi(act, 1, 1)
                if t >= 1:
                    turn_hi(norm0, t - 1, x_hi)
            turn_hi(norm0, NT - 1, x_hi)
            load_gains(act, norm1, "ffn1_post_g", "mix_pre_g")
            ffn_act(act, uses, 0, True)

            act.wait_ge(w_full[2], CHUNKS)
            for t in range(2):
                load_resid(act, norm1, resid_a, x_in, t)

            def u_tile(t):
                act.wait_ge(mix["full"], t + 1)
                if t == 0:
                    act.wait_ge(norm1["stored0"], 16 * PAIRS)
                act.activation(u_sb[:, t, :], bank(t % 4), ACT.Gelu_apprx_tanh).then_inc(mix["u"], 1)

            for p in range(PAIRS):
                for t in (2 * p, 2 * p + 1):
                    act.wait_ge(ffn["y"], 2 * NT * (CHUNKS - 1) + 2 * t + 2)
                    square_y(norm1, t)
                for t in (2 * p, 2 * p + 1):
                    square_h(norm1, t, h_dram[0], resid_a, x_in)
                for t in (2 * p, 2 * p + 1):
                    if t == 0:
                        act.wait_ge(ffn["gu"], 8 * CHUNKS)
                    turn_hi(norm1, t, x_hi)
                if p >= 2:
                    for t in (2 * p - 4, 2 * p - 3):
                        u_tile(t)
            for t in (NT - 4, NT - 3):
                u_tile(t)
            next_hi(act, uses, 0, mix["half"], 1)
            for t in (NT - 2, NT - 1):
                u_tile(t)
            next_hi(act, uses, 1, mix["full"], NT)
            act.wait_ge(mix["ws_turned"], 1)
            act.activation(ws_t[:, :, :], bank(6).rearrange("p (g t) -> p g t", g=G), ACT.Copy).then_inc(mix["ws"], 1)
            for t in range(NT):
                if t == NT - 2:
                    next_hi(act, uses, 0, mix["half"], 2)
                act.wait_ge(mix["full"], NT + t + 1)
                act.activation(vg[:, t, :], bank(t % 4), ACT.Gelu_apprx_tanh).then_inc(mix["vg"], 1)
            next_hi(act, uses, 1, mix["full"], 2 * NT)
            for t in range(NT):
                if t == NT - 2:
                    next_hi(act, uses, 0, mix["half"], 3)
                act.wait_ge(mix["full"], 2 * NT + t + 1)
                act.activation(v_sb[:, t, :], bank(t % 4), ACT.Copy).then_inc(mix["v_done"], 1)
            next_hi(act, uses, 1, mix["full"], 3 * NT)
            act.wait_ge(norm1["stored1"], 16 * PAIRS)
            act.wait_ge(mix["mixed"], NT)
            for b in range(QK_BLOCKS):
                for n in range(4):
                    idx = 4 * b + n
                    tile, h = idx // 2, idx % 2
                    at = slice(h * HALF, (h + 1) * HALF)
                    act.wait_ge(mix["qk"], idx + 1)
                    if b < QK_BLOCKS // 2:
                        for dst, rows in ((q_even, slice(0, HD)), (q_odd, slice(HD, P))):
                            act.activation(dst[rows, tile, at], bank(idx % 4)[rows, :], ACT.Copy, scale=HD ** -0.5)\
                               .then_inc(mix["qk_done"], 1)
                    else:
                        act.activation(k_t[:, tile - SBW // P, at], bank(idx % 4), ACT.Copy).then_inc(mix["qk_done"], 2)
                next_hi(act, uses, b % 2, mix["qk"], 4 * b + 4)

            def merge_squares(t):
                act.wait_ge(mix["out_a"], G * (t + 1))
                square_sum(u_sb[:, t, :], t, merge["sum_y"], t + 1, SW)
                act.wait_ge(sb_att["out_b"], t + 1)
                square_sum(out_b[:, :, t * P:(t + 1) * P], NT + t, merge["sum_h"], t + 1, SBW, P)

            for n in range(N_ATT + 2):
                if n < N_ATT:
                    u, W = n % 2, (n // SBH + 1) * P
                    z = bank(2 * u, 2)[:, 0:W]
                    act.wait_ge(sb_att["z"], n + 1)
                    if n >= 2:
                        act.wait_ge(sb_att["turned"], n - 1)
                    act.activation(beta[:, u, 0:W], z, ACT.Sigmoid).then_inc(sb_att["beta"], 1)
                    act.activation(keep[:, u, 0:W], z, ACT.Sigmoid, scale=-1.0).then_inc(sb_att["keep"], 1)
                if n >= 2:
                    m = n - 2
                    W = (m // SBH + 1) * P
                    act.wait_ge(sb_att["turned"], m + 1)
                    if m >= 2:
                        act.wait_ge(sb_att["av"], m - 1)
                    act.activation(attn_t[:, m % 2, 0:W], bank(4, 2)[:, 0:W], ACT.Copy).then_inc(sb_att["attn_t"], 1)
                if n >= SBH + 5 and (n - 5) % SBH == 0:
                    merge_squares((n - 5) // SBH - 1)
            act.dma_start(gain_pre[:, 0:SW], a["sgu_out_g"].broadcast_to((P, SW))).then_inc(merge["gains"], 16)
            act.dma_start(gain_pre[:, SW:D], a["sb_out_g"].broadcast_to((P, SBW))).then_inc(merge["gains"], 16)
            act.dma_start(gain_post[:, :], a["mem_norm_g"].broadcast_to((P, D))).then_inc(norm_mem["gains"], 16)
            act.wait_ge(sb_att["av"], N_ATT)
            for t in range(NM):
                load_resid(act, norm_mem, resid_b, a["mem"][0], t)
            merge_squares(NT - 1)

            for t in range(NT):
                turn_hi(merge, t, x_hi)
            for t in range(NM):
                wait_resid(act, norm_mem, t)
                square_sum(resid_b[:, t, :], NT + t, norm_mem["sum_h"], t + 1)
            for t in range(NT):
                if t == NT - 2:
                    next_hi(act, uses, 0, wout["half"], 1)
                project_y(wout, 0, t)
            next_hi(act, uses, 1, wout["full"], NT)
            for t in range(NM):
                turn_hi(norm_mem, t, m_hi)
            act.wait_ge(norm_mem["normed"], NM)
            load_gains(act, norm2, "mix_post_g", "xa_pre_g")
            act.wait_ge(norm1["stored0"], 16 * PAIRS)
            for t in range(2):
                load_resid(act, norm2, resid_b, h_dram[0], t)

            for p in range(PAIRS):
                if p == PAIRS - 1:
                    next_hi(act, uses, 0, wout["half"], 2)
                for t in (2 * p, 2 * p + 1):
                    project_y(wout, 1, t)
                if p == PAIRS - 1:
                    next_hi(act, uses, 1, wout["full"], 2 * NT)
                norm_pair(norm2, p, wout["y"], h_dram[1], resid_b, h_dram[0])
            for b in range(XK_BLOCKS):
                for c in range(2):
                    act.wait_ge(xkv["k"], 2 * b + c + 1)
                    act.activation(mem_k[:, 2 * b + c, :], bank((2 * b + c) % 4)[:, 0:M], ACT.Copy)\
                       .then_inc(xkv["k_done"], 1)
                next_hi(act, uses, b % 2, xkv["k"], 2 * b + 2)
            for cb in range(2):
                next_hi(act, uses, 0, xkv["half"], cb + 1)
                for t in range(NM):
                    act.wait_ge(xkv["v"], cb * NM + t + 1)
                    act.activation(mem_v[:, t, cb * BANK:(cb + 1) * BANK], bank(2 * cb + t), ACT.Copy)\
                       .then_inc(xkv["v_done"], 1)
                next_hi(act, uses, 1, xkv["v"], (cb + 1) * NM)
            for u in range(2):
                act.wait_ge(norm2[f"stored{u}"], 16 * PAIRS)
            for b in range(XK_BLOCKS):
                for n in range(4):
                    idx = 4 * b + n
                    tile, h = idx // 2, idx % 2
                    act.wait_ge(xq["q"], idx + 1)
                    act.activation(xq_t[:, tile, h * HALF:(h + 1) * HALF], bank(idx % 4), ACT.Copy).then_inc(xq["q_done"], 1)
                next_hi(act, uses, b % 2, xq["q"], 4 * b + 4)
            for t in range(2):
                load_resid(act, norm3, resid_b, h_dram[1], t)

            def o_hi(t):
                act.wait_ge(xatt["o"], t + 1)
                act.activation(x_hi[:, :, t * P:(t + 1) * P], bank(6, 2).rearrange("p (k c) -> p k c", c=P),
                               ACT.Copy).then_inc(xatt["o_hi"], 1)

            def o_projected(t):
                act.wait_ge(xo["full"], t + 1)
                if t == 0:
                    act.wait_ge(xatt["logits"], NT)
                act.activation(y[:, t, 0:BANK], bank(2 + t % 2), ACT.Copy).then_inc(xo["y"], 1)

            for t in range(NT):
                u = t % 2
                act.wait_ge(xatt["neg"], t + 1)
                if t >= 2:
                    act.wait_ge(xatt["turned"], t - 1)
                for h in range(XHEADS):
                    act.activation(probs[:, u, h, :], bank(0, 2)[:, h * M:(h + 1) * M], ACT.Exp,
                                   bias=small[:, 48 + 4 * u + h:49 + 4 * u + h], scale=XHD ** -0.5,
                                   accum_out=small[:, 56 + 4 * u + h:57 + 4 * u + h]).then_inc(xatt["probs"], 1)
                if t >= 1:
                    o_hi(t - 1)
            o_hi(NT - 1)
            load_gains(act, norm3, "xa_post_g", "ffn2_pre_g")
            for t in range(NT):
                if t == NT - 1:
                    next_hi(act, uses, 0, xo["half"], 1)
                o_projected(t)
            next_hi(act, uses, 1, xo["full"], NT)
            for p in range(PAIRS):
                if p == PAIRS - 1:
                    next_hi(act, uses, 0, xo["half"], 2)
                for t in (2 * p, 2 * p + 1):
                    project_y(xo, 1, t)
                if p == PAIRS - 1:
                    next_hi(act, uses, 1, xo["full"], 2 * NT)
                norm_pair(norm3, p, xo["y"], h_dram[2], resid_b, h_dram[1])
            load_gains(act, norm4, "ffn2_post_g", "final_norm_g")
            ffn_act(act, uses, CHUNKS, False)

            act.wait_ge(w_full[2], 2 * CHUNKS)
            for t in range(2):
                load_resid(act, norm4, resid_a, h_dram[2], t)
            for p in range(PAIRS):
                for t in (2 * p, 2 * p + 1):
                    act.wait_ge(ffn["y"], 2 * NT * (2 * CHUNKS - 1) + 2 * t + 2)
                    square_y(norm4, t)
                for t in (2 * p, 2 * p + 1):
                    square_h(norm4, t, None, resid_a, h_dram[2])
                for t in (2 * p, 2 * p + 1):
                    act.wait_ge(norm4["rstd_h"], t + 1)
                    act.activation(y[:, t, :], y[:, t, :], ACT.Copy, scale=rstd[:, NT + t:NT + t + 1])\
                       .then_inc(norm4["unit"], 1)

        def split_lo(dve, s, n):
            dve.wait_ge(hi_done[s], n)
            dve.tensor_tensor(lo(s), raw(s), hi(s).bitcast(F32), ALU.subtract).then_inc(w_full[s], 1)

        def next_lo(dve, uses, s):
            uses.n[s] += 1
            split_lo(dve, s, uses.n[s])

        def post_norm(dve, s, t, c, place):
            if t == 0:
                dve.wait_ge(s["gains"], 32)
            dve.wait_ge(s["rstd_y"], t + 1)
            dve.scalar_tensor_tensor(y[:, t, :], y[:, t, :], rstd[:, t:t + 1], gain_post[:, :], ALU.mult, ALU.mult)\
               .then_inc(s["scaled"], 1)
            dve.wait_ge(s["scaled"], t + 1)
            wait_resid(dve, s, t)
            dve.scalar_tensor_tensor(y[:, t, :], y[:, t, :], c, place[:, t % 2, :], ALU.mult, ALU.add)\
               .then_inc(s["h"], 1)

        def pre_norm(dve, s, t, src, gain):
            if t >= 2:
                dve.wait_ge(s["turned"], t - 1)
            dve.wait_ge(s["rstd_h"], t + 1)
            dve.scalar_tensor_tensor(normed[:, t % 2, :], src, rstd[:, NT + t:NT + t + 1], gain, ALU.mult, ALU.mult)\
               .then_inc(s["normed"], 1)

        def turn_lo(dve, s, t, dst_hi, dst_lo):
            dve.wait_ge(s["x_hi"], t + 1)
            at = slice(t * P, (t + 1) * P)
            dve.tensor_tensor(dst_lo[:, :, at], turn_bank(t).rearrange("p (k c) -> p k c", c=P),
                              dst_hi[:, :, at].bitcast(F32), ALU.subtract).then_inc(s["x_full"], 1)

        def norm_pair_dve(dve, s, p, c, place):
            pair = (2 * p, 2 * p + 1)
            for t in pair:
                post_norm(dve, s, t, c, place)
            for t in pair:
                pre_norm(dve, s, t, y[:, t, :], gain_pre[:, :])
            for t in pair:
                turn_lo(dve, s, t, x_hi, x_lo)

        def ffn_dve(dve, uses, c0, prefetch_last, first_y, last_y):
            def hidden(i, q):
                f, h = q % 2, q // 2
                idx = 4 * i + q
                dve.wait_ge(ffn["gate_act"], idx + 1)
                dve.wait_ge(ffn["gu"], 2 * idx + 2)
                dve.tensor_tensor(product[:, q % 2, :], gate_act[:, q % 2, :], bank(2 * (q % 2) + 1), ALU.mult)\
                   .then_inc(ffn["product"], 1)
                dve.wait_ge(ffn["hid_hi"], idx + 1)
                at = slice(h * HALF, (h + 1) * HALF)
                dve.tensor_tensor(hid_lo[:, f, at], product[:, q % 2, :], hid_hi[:, f, at].bitcast(F32),
                                  ALU.subtract).then_inc(ffn["hid_full"], 1)

            def chunk(i, first, last):
                hidden(i, 0)
                split_lo(dve, 2, uses.n[2] + 1 - c0 + i)
                hidden(i, 1)
                hidden(i, 2)
                if prefetch_last or not last:
                    split_lo(dve, 0, uses.n[0] + 1 - c0 + i)
                hidden(i, 3)
                if first:
                    first_y()
                else:
                    dve.wait_ge(ffn["y"], 2 * NT * i)

                def add(t):
                    for h in range(2):
                        n = 2 * t + h
                        dve.wait_ge(ffn["down"], 2 * NT * i + n + 1)
                        acc = y[:, t, h * BANK:(h + 1) * BANK]
                        if first:
                            op = dve.tensor_copy(acc, bank(4 + n % 4))
                        else:
                            op = dve.tensor_tensor(acc, acc, bank((4 + n) % 8 if last else 4 + n % 4), ALU.add)
                        op.then_inc(ffn["y"], 1)
                if last:
                    last_y(add)
                else:
                    for t in range(NT):
                        add(t)
                if not last:
                    split_lo(dve, 1, uses.n[1] + 1 - c0 + i)

            chunk(c0, True, False)
            with dve.Fori(c0 + 1, c0 + CHUNKS - 1) as i:
                chunk(i, False, False)
            chunk(c0 + CHUNKS - 1, False, True)
            uses.n[2] += CHUNKS
            uses.n[0] += CHUNKS - (not prefetch_last)
            uses.n[1] += CHUNKS - 1

        @block.vector
        def _(dve):
            uses = Uses()
            dve.wait_ge(norm0["gains"], 16)
            for t in range(NT):
                pre_norm(dve, norm0, t, y[:, t, :], gain_pre[:, :])
                if t == 3:
                    next_lo(dve, uses, 0)
                if t == 5:
                    next_lo(dve, uses, 1)
                if t >= 1:
                    turn_lo(dve, norm0, t - 1, x_hi, x_lo)
            turn_lo(dve, norm0, NT - 1, x_hi, x_lo)

            def sums_and_norm1(add):
                add(0)
                add(1)
                post_norm(dve, norm1, 0, 0.5, resid_a)
                add(2)
                post_norm(dve, norm1, 1, 0.5, resid_a)
                add(3)
                pre_norm(dve, norm1, 0, y[:, 0, :], gain_pre[:, :])
                add(4)
                pre_norm(dve, norm1, 1, y[:, 1, :], gain_pre[:, :])
                add(5)
                turn_lo(dve, norm1, 0, x_hi, x_lo)
                add(6)
                turn_lo(dve, norm1, 1, x_hi, x_lo)
                add(7)
                next_lo(dve, uses_last, 1)
                for p in range(1, PAIRS):
                    norm_pair_dve(dve, norm1, p, 0.5, resid_a)

            uses_last = Uses()
            uses_last.n[1] = CHUNKS
            ffn_dve(dve, uses, 0, True, lambda: None, sums_and_norm1)
            uses.n[1] = uses_last.n[1]
            next_lo(dve, uses, 0)
            next_lo(dve, uses, 1)

            def centre(t):
                stats = small[:, 64:64 + 6 * G].rearrange("p (g six) -> p g six", six=6)
                mean_var = small[:, 32 + 8 * (t % 2):40 + 8 * (t % 2)].rearrange("p (g two) -> p g two", two=2)
                dve.wait_ge(mix["vg"], t + 1)
                if t:
                    dve.wait_ge(mix["stats"], G * t)
                for g in range(G):
                    dve.bn_stats(stats[:, g, :], vg[:, t, g * GD:(g + 1) * GD]).then_inc(mix["bn"], 1)
                if t >= 2:
                    dve.wait_ge(mix["centred"], G * (t - 1))
                for g in range(G):
                    dve.wait_ge(mix["bn"], G * t + g + 1)
                    dve.bn_aggr(mean_var[:, g, :], stats[:, g, :]).then_inc(mix["stats"], 1)

            def gain(t):
                mean_var = small[:, 32 + 8 * (t % 2):40 + 8 * (t % 2)].rearrange("p (g two) -> p g two", two=2)
                if t == 0:
                    dve.wait_ge(mix["const"], 48)
                dve.wait_ge(mix["rstd"], t + 1)
                for g in range(G):
                    at = vg[:, t, g * GD:(g + 1) * GD]
                    dve.tensor_scalar(at, at, mean_var[:, g, 0:1], mean_var[:, g, 1:2], ALU.subtract, ALU.mult)\
                       .then_inc(mix["centred"], 1)
                dve.wait_ge(mix["centred"], G * (t + 1))
                dve.tensor_tensor(vg[:, t, :], vg[:, t, :], sgu_bc[:, 0, :], ALU.mult).then_inc(mix["gained"], 1)
                dve.wait_ge(mix["gained"], t + 1)
                dve.tensor_tensor(vg[:, t, :], vg[:, t, :], sgu_bc[:, 1, :], ALU.add).then_inc(mix["vn"], 1)

            def gate(t):
                dve.wait_ge(mix["mixed"], t + 1)
                for g in range(G):
                    at = slice(g * GD, (g + 1) * GD)
                    dve.scalar_tensor_tensor(u_sb[:, t, at], bank(4 + t % 2)[:, at], small[:, g:g + 1], u_sb[:, t, at],
                                             ALU.add, ALU.mult).then_inc(mix["out_a"], 1)

            for t in range(NT):
                centre(t)
                if t >= 1:
                    gain(t - 1)
                if t == NT - 1:
                    next_lo(dve, uses, 0)
            next_lo(dve, uses, 1)
            gain(NT - 1)
            for t in range(NT):
                gate(t)
                if t == NT - 3:
                    next_lo(dve, uses, 0)
            next_lo(dve, uses, 1)
            for b in range(QK_BLOCKS):
                next_lo(dve, uses, b % 2)

            dve.wait_ge(mix["qk"], 4 * QK_BLOCKS)
            dve.memset(suffix[:, :, :], 1.0).then_inc(sb_att["ones"], 1)
            dve.wait_ge(sb_att["ones"], 1)

            def out_b_tile(i):
                dve.wait_ge(sb_att["av"], SBH * (i + 1))
                dve.tensor_copy(out_b[:, :, i * P:(i + 1) * P], bank(6 + i % 2).rearrange("p (c d) -> p c d", d=P))\
                   .then_inc(sb_att["out_b"], 1)

            for n in range(N_ATT):
                u, W = n % 2, (n // SBH + 1) * P
                dve.wait_ge(sb_att["keep"], n + 1)
                if n >= 2:
                    dve.wait_ge(sb_att["attn"], n - 1)
                backwards = keep[:, u, 0:W][:, ::-1]
                dve.tensor_tensor_scan(suffix[:, u, 0:W][:, ::-1], backwards, backwards, 1.0, ALU.mult, ALU.bypass)\
                   .then_inc(sb_att["suffix"], 1)
                dve.wait_ge(sb_att["suffix"], n + 1)
                dve.tensor_tensor(beta[:, u, 0:W], beta[:, u, 0:W], suffix[:, u, 1:W + 1], ALU.mult)\
                   .then_inc(sb_att["attn"], 1)
                if n >= SBH + 2 and (n - 2) % SBH == 0:
                    out_b_tile((n - 2) // SBH - 1)
            out_b_tile(NT - 1)

            dve.wait_ge(merge["gains"], 32)

            def merge_tile(t):
                u = t % 2
                if t >= 2:
                    dve.wait_ge(merge["turned"], t - 1)
                dve.wait_ge(merge["rstd_y"], t + 1)
                dve.scalar_tensor_tensor(normed[:, u, 0:SW], u_sb[:, t, :], rstd[:, t:t + 1], gain_pre[:, 0:SW],
                                         ALU.mult, ALU.mult).then_inc(merge["left"], 1)
                dve.wait_ge(merge["rstd_h"], t + 1)
                dve.scalar_tensor_tensor(normed[:, u, SW:D].rearrange("p (c d) -> p c d", d=P),
                                         out_b[:, :, t * P:(t + 1) * P], rstd[:, NT + t:NT + t + 1],
                                         gain_pre[:, SW:D].rearrange("p (c d) -> p c d", d=P), ALU.mult, ALU.mult)\
                   .then_inc(merge["normed"], 1)

            for p in range(PAIRS):
                for t in (2 * p, 2 * p + 1):
                    merge_tile(t)
                for t in (2 * p, 2 * p + 1):
                    turn_lo(dve, merge, t, x_hi, x_lo)
            dve.wait_ge(norm_mem["gains"], 16)
            dve.wait_ge(merge["turned"], NT)
            for t in range(NM):
                pre_norm(dve, norm_mem, t, resid_b[:, t, :], gain_post[:, :])
            next_lo(dve, uses, 0)
            next_lo(dve, uses, 1)
            for t in range(NM):
                turn_lo(dve, norm_mem, t, m_hi, m_lo)
            for p in range(PAIRS - 1):
                norm_pair_dve(dve, norm2, p, 1.0, resid_b)
            next_lo(dve, uses, 0)
            next_lo(dve, uses, 1)
            norm_pair_dve(dve, norm2, PAIRS - 1, 1.0, resid_b)
            for _ in range(XK_BLOCKS // 2 + 2 + XK_BLOCKS // 2):
                next_lo(dve, uses, 0)
                next_lo(dve, uses, 1)

            def o_lo(t):
                dve.wait_ge(xatt["o_hi"], t + 1)
                at = slice(t * P, (t + 1) * P)
                dve.tensor_tensor(x_lo[:, :, at], bank(6, 2).rearrange("p (k c) -> p k c", c=P),
                                  x_hi[:, :, at].bitcast(F32), ALU.subtract).then_inc(xatt["o_full"], 1)

            for t in range(NT):
                u = t % 2
                m0, n0, r0, s0 = 32 + 4 * u, 48 + 4 * u, 40 + 4 * u, 56 + 4 * u
                dve.wait_ge(xatt["logits"], t + 1)
                if t >= 2:
                    dve.wait_ge(xatt["neg"], t - 1)
                dve.tensor_reduce(small[:, m0:m0 + 4], bank(0, 2).rearrange("p (h m) -> p h m", m=M), AX.X, ALU.max)\
                   .then_inc(xatt["max"], 1)
                dve.wait_ge(xatt["max"], t + 1)
                if t >= 2:
                    dve.wait_ge(xatt["probs"], XHEADS * (t - 1))
                dve.tensor_scalar(small[:, n0:n0 + 4], small[:, m0:m0 + 4], -(XHD ** -0.5), None, ALU.mult)\
                   .then_inc(xatt["neg"], 1)
                dve.wait_ge(xatt["probs"], XHEADS * (t + 1))
                if t >= 2:
                    dve.wait_ge(xatt["scaled"], XHEADS * (t - 1))
                dve.reciprocal(small[:, r0:r0 + 4], small[:, s0:s0 + 4]).then_inc(xatt["recip"], 1)
                dve.wait_ge(xatt["recip"], t + 1)
                for h in range(XHEADS):
                    dve.tensor_scalar(probs[:, u, h, :], probs[:, u, h, :], small[:, r0 + h:r0 + h + 1], None,
                                      ALU.mult).then_inc(xatt["scaled"], 1)
                if t >= 1:
                    o_lo(t - 1)
                dve.wait_ge(xatt["turned"], t + 1)
                dve.tensor_copy(probs_t[:, :], bank(4, 2)).then_inc(xatt["probs_t"], 1)
            o_lo(NT - 1)
            next_lo(dve, uses, 0)
            next_lo(dve, uses, 1)
            for p in range(PAIRS - 1):
                norm_pair_dve(dve, norm3, p, 1.0, resid_b)
            next_lo(dve, uses, 0)
            next_lo(dve, uses, 1)
            norm_pair_dve(dve, norm3, PAIRS - 1, 1.0, resid_b)

            def h_stored():
                for u in range(2):
                    dve.wait_ge(norm3[f"stored{u}"], 16 * PAIRS)

            def sums_and_norm4(add):
                add(0)
                add(1)
                for t in range(NT):
                    post_norm(dve, norm4, t, 0.5, resid_a)
                    if t + 2 < NT:
                        add(t + 2)
            ffn_dve(dve, uses, CHUNKS, False, h_stored, sums_and_norm4)

        def split3(pe, dst, lh, ll, rh, rl, first, last):
            pe.matmul(dst, lh, rh, start=first, stop=False)
            pe.matmul(dst, lh, rl, start=False, stop=False)
            return pe.matmul(dst, ll, rh, start=False, stop=last)

        def turn(pe, s, t):
            pe.wait_ge(s["normed"], t + 1)
            if t >= 2:
                pe.wait_ge(s["x_full"], t - 1)
            for k in range(NK):
                mm = pe.transpose(turn_bank(t)[:, k * P:(k + 1) * P], normed[:, t % 2, k * P:(k + 1) * P], ident[:, :])
            mm.then_inc(s["turned"], 1)

        def rows_part(pe, b, t, s, src_hi, src_lo):
            for k in range(4):
                kk = 4 * s + k
                mm = split3(pe, bank(b), src_hi[:, kk, t * P:(t + 1) * P], src_lo[:, kk, t * P:(t + 1) * P],
                            hi(s)[:, k * BANK:(k + 1) * BANK], lo(s)[:, k * BANK:(k + 1) * BANK],
                            s == 0 and k == 0, s == 1 and k == 3)
            return mm

        def rows_pair(pe, uses, st, p, tiles, banks, wait, between):
            a_, b_ = tiles
            last = p == "last"
            for s in range(2):
                pe.wait_ge(w_full[s], uses.n[s] + 1)
                for j, t in enumerate((a_, b_)):
                    if s == 0:
                        wait(t)
                    mm = rows_part(pe, banks[j], t, s, *st["src"])
                    if s == 0 and j == 1 and last:
                        mm.then_inc(st["half"], 1)
                    if s == 1:
                        mm.then_inc(st["full"], 1)
                    between(2 * s + j)
            if last:
                for s in range(2):
                    uses.n[s] += 1

        def ffn_pe(pe, uses, c0, x_full, banks_free, between, turn_late):
            def chunk(i, first, last):
                for q in range(4):
                    f, h = q % 2, q // 2
                    if q < 2:
                        pe.wait_ge(w_full[f], uses.n[f] + 1 - c0 + i)
                    if first and q % 2 == 0:
                        pe.wait_ge(x_full, NT // 2 * (h + 1))
                    if first and q == 0:
                        banks_free()
                    if not (first and q < 2):
                        pe.wait_ge(ffn["product"], 4 * i + q - 1)
                    for g in range(2):
                        for k in range(NK):
                            at = slice((g * NK + k) * P, (g * NK + k + 1) * P)
                            half = slice(h * HALF, (h + 1) * HALF)
                            mm = split3(pe, bank(2 * (q % 2) + g), hi(f)[:, at], lo(f)[:, at],
                                        x_hi[:, k, half], x_lo[:, k, half], k == 0, k == NK - 1)
                        mm.then_inc(ffn["gu"], 1)
                        if first:
                            between(2 * q + g)
                pe.wait_ge(w_full[2], uses.n[2] + 1 - c0 + i)
                for t in range(NT):
                    if t % (NT // 2) == 0:
                        pe.wait_ge(ffn["hid_full"], 4 * i + 2 + t // (NT // 2) * 2)
                    for h in range(2):
                        n = 2 * t + h
                        if last and n in (4, 6):
                            pe.wait_ge(ffn["product"], 4 * i + 3 + (n == 6))
                        if last and n >= 8:
                            pe.wait_ge(ffn["y"], 2 * NT * i + n - 7)
                        elif not (first and n < 4) and not (last and n >= 4):
                            pe.wait_ge(ffn["y"], 2 * NT * i + n - 3)
                        for f in range(2):
                            at = slice(f * D + h * BANK, f * D + (h + 1) * BANK)
                            mm = split3(pe, bank((4 + n) % 8 if last else 4 + n % 4), hid_hi[:, f, t * P:(t + 1) * P],
                                        hid_lo[:, f, t * P:(t + 1) * P], w2_hi[:, at], w2_lo[:, at], f == 0, f == 1)
                        mm.then_inc(ffn["down"], 1)
                    if last:
                        turn_late(t)

            chunk(c0, True, False)
            with pe.Fori(c0 + 1, c0 + CHUNKS - 1) as i:
                chunk(i, False, False)
            chunk(c0 + CHUNKS - 1, False, True)
            for f in range(3):
                uses.n[f] += CHUNKS

        def cols_group(pe, b, s, c, width, h, src_hi, src_lo):
            for k in range(NK):
                at = slice(k * COLS + c * P, k * COLS + (c + 1) * P)
                mm = split3(pe, bank(b)[:, 0:width], hi(s)[:, at], lo(s)[:, at],
                            src_hi[:, k, h * width:(h + 1) * width], src_lo[:, k, h * width:(h + 1) * width],
                            k == 0, k == NK - 1)
            return mm

        @block.tensor
        def _(pe):
            uses = Uses()
            nothing = lambda *_: None
            pe.wait_ge(const["made"], 3)
            for t in range(4):
                turn(pe, norm0, t)

            def x_turns(n):
                if n < 4:
                    turn(pe, norm0, 4 + n)

            ffn_end = 2 * NT * (CHUNKS - 1)

            def norm1_turns(t):
                if t == 5:
                    pe.wait_ge(ffn["y"], ffn_end + 10)
                    turn(pe, norm1, 0)
                if t == 6:
                    pe.wait_ge(ffn["y"], ffn_end + 12)
                    turn(pe, norm1, 1)

            ffn_pe(pe, uses, 0, norm0["x_full"], nothing, x_turns, norm1_turns)
            pe.wait_ge(ffn["y"], ffn_end + 16)

            def pairs(st, cb, wait, between=nothing):
                for p in range(PAIRS):
                    rows_pair(pe, uses, st, "last" if p == PAIRS - 1 else p, (2 * p, 2 * p + 1),
                              (2 * p % 4, 2 * p % 4 + 1), wait, lambda n: between(p, n))

            x_mix = {"src": (x_hi, x_lo), "half": mix["half"], "full": mix["full"]}

            def behind(s, p, n):
                if n in (1, 2) and p < PAIRS - 1:
                    turn(pe, s, 2 * p + 1 + n)

            def u_wait(t):
                pe.wait_ge(norm1["x_full"], 2 * (t // 2) + 2)
                if t >= 4:
                    pe.wait_ge(mix["u"], t - 3)

            pairs(x_mix, 0, u_wait, lambda p, n: behind(norm1, p, n))
            pe.wait_ge(mix["masked"], 1)
            for g in range(G):
                mm = pe.transpose(bank(6)[:, g * P:(g + 1) * P], ws_raw[:, g, :], ident[:, :])
            mm.then_inc(mix["ws_turned"], 1)
            pairs(x_mix, 1, lambda t: pe.wait_ge(mix["u"], t + 5) if t < 4 else pe.wait_ge(mix["vg"], t - 3))

            def causal_mix(p, n):
                if n == 1 and p == 0:
                    pe.wait_ge(mix["ws"], 1)
                if n in (1, 3):
                    t = 2 * p + n // 2
                    pe.wait_ge(mix["vn"], t + 1)
                    if t >= 2:
                        pe.wait_ge(mix["out_a"], G * (t - 1))
                    for g in range(G):
                        at = slice(g * GD, (g + 1) * GD)
                        mm = pe.matmul(bank(4 + t % 2)[:, at], ws_t[:, g, :], vg[:, t, at], start=True, stop=True)
                    mm.then_inc(mix["mixed"], 1)

            pairs(x_mix, 2, lambda t: pe.wait_ge(mix["vg"], t + 5) if t < 4 else pe.wait_ge(mix["v_done"], t - 3),
                  causal_mix)
            for b in range(QK_BLOCKS):
                s = b % 2
                pe.wait_ge(w_full[s], uses.n[s] + 1)
                for n in range(4):
                    idx = 4 * b + n
                    if idx < 4:
                        pe.wait_ge(mix["v_done"], idx + 5)
                    else:
                        pe.wait_ge(mix["qk_done"], 2 * (idx - 3))
                    cols_group(pe, idx % 4, s, n // 2, BANK, n % 2, x_hi, x_lo).then_inc(mix["qk"], 1)
                uses.n[s] += 1

            def scores(n):
                i, h = divmod(n, SBH)
                W = (i + 1) * P
                if n >= 2:
                    pe.wait_ge(sb_att["keep"], n - 1)
                q = (q_even, q_odd)[h % 2]
                z = bank(2 * (n % 2), 2)
                for c in range(0, W, BANK):
                    c1 = min(W, c + BANK)
                    mm = pe.matmul(z[:, c:c1], q[:, h // 2, i * P:(i + 1) * P], k_t[:, h // 2, c:c1],
                                   start=True, stop=c1 < W)
                pe.matmul(z[:, W - P:W], ident_bf[:, :], causal_neg[:, :], start=False, stop=True)\
                  .then_inc(sb_att["z"], 1)

            def turns(n):
                pe.wait_ge(sb_att["attn"], n + 1)
                if n >= 1:
                    pe.wait_ge(sb_att["attn_t"], n)
                for j in range(n // SBH + 1):
                    mm = pe.transpose(bank(4, 2)[:, j * P:(j + 1) * P], beta[:, n % 2, j * P:(j + 1) * P], ident[:, :])
                mm.then_inc(sb_att["turned"], 1)

            def values(n):
                i, h = divmod(n, SBH)
                pe.wait_ge(sb_att["attn_t"], n + 1)
                if h == 0 and i >= 2:
                    pe.wait_ge(sb_att["out_b"], i - 1)
                for j in range(i + 1):
                    mm = pe.matmul(bank(6 + i % 2)[:, h * HD:(h + 1) * HD], attn_t[:, n % 2, j * P:(j + 1) * P],
                                   v_sb[:, j, h * HD:(h + 1) * HD], start=j == 0, stop=j == i)
                mm.then_inc(sb_att["av"], 1)

            pe.wait_ge(mix["qk_done"], 8 * QK_BLOCKS)
            pe.wait_ge(mix["padded"], 2)
            pe.wait_ge(mix["out_a"], G * NT)
            scores(0)
            for n in range(N_ATT + 2):
                if n + 1 < N_ATT:
                    scores(n + 1)
                if 1 <= n <= N_ATT:
                    turns(n - 1)
                if n >= 2:
                    values(n - 2)

            pe.wait_ge(sb_att["out_b"], NT)
            for t in range(2):
                turn(pe, merge, t)

            def wout_between(p, n):
                if p == 0:
                    behind(merge, p, n)
                if p == 1 and n >= 1:
                    for t in {1: (4,), 2: (5,), 3: (6, 7)}[n]:
                        turn(pe, merge, t)
                if p == PAIRS - 1 and n in (1, 2):
                    if n == 1:
                        pe.wait_ge(merge["x_full"], NT)
                    turn(pe, norm_mem, n - 1)

            x_wout = {"src": (x_hi, x_lo), "half": wout["half"], "full": wout["full"]}

            def wout_wait(t):
                pe.wait_ge(merge["x_full"], 2 * (t // 2) + 2)
                if t >= 4:
                    pe.wait_ge(wout["y"], t - 3)

            pairs(x_wout, 0, wout_wait, wout_between)

            def ahead(s, p, n):
                if n in (2, 3) and p > 0:
                    turn(pe, s, 2 * p - 4 + n)

            pe.wait_ge(norm_mem["x_full"], NM)
            pairs(x_wout, 1, lambda t: pe.wait_ge(wout["y"], NT + t - 3), lambda p, n: ahead(norm2, p, n))

            for b in range(XK_BLOCKS):
                s = b % 2
                pe.wait_ge(w_full[s], uses.n[s] + 1)
                for c in range(2):
                    idx = 2 * b + c
                    if idx < 4:
                        pe.wait_ge(wout["y"], 2 * NT - 3 + idx)
                    else:
                        pe.wait_ge(xkv["k_done"], idx - 3)
                    cols_group(pe, idx % 4, s, c, M, 0, m_hi, m_lo).then_inc(xkv["k"], 1)
                    if idx in (2, 3):
                        turn(pe, norm2, NT - 4 + idx)
                uses.n[s] += 1
            x_mem = {"src": (m_hi, m_lo), "half": xkv["half"], "full": xkv["v"]}
            for cb in range(2):
                rows_pair(pe, uses, x_mem, "last", (0, 1), (2 * cb, 2 * cb + 1),
                          lambda t: pe.wait_ge(xkv["k_done"], 2 * XK_BLOCKS - 3 + 2 * cb + t), nothing)
            pe.wait_ge(norm2["x_full"], NT)
            for b in range(XK_BLOCKS):
                s = b % 2
                pe.wait_ge(w_full[s], uses.n[s] + 1)
                for n in range(4):
                    idx = 4 * b + n
                    if idx < 4:
                        pe.wait_ge(xkv["v_done"], idx + 1)
                    else:
                        pe.wait_ge(xq["q_done"], idx - 3)
                    cols_group(pe, idx % 4, s, n // 2, BANK, n % 2, x_hi, x_lo).then_inc(xq["q"], 1)
                uses.n[s] += 1

            def logits(t):
                if t == 0:
                    pe.wait_ge(xq["q_done"], 4 * XK_BLOCKS)
                else:
                    pe.wait_ge(xatt["probs"], XHEADS * t)
                for h in range(XHEADS):
                    for c in range(2):
                        mm = pe.matmul(bank(0, 2)[:, h * M:(h + 1) * M], xq_t[:, 2 * h + c, t * P:(t + 1) * P],
                                       mem_k[:, 2 * h + c, :], start=c == 0, stop=c == 1)
                mm.then_inc(xatt["logits"], 1)

            def turn_probs(t):
                pe.wait_ge(xatt["scaled"], XHEADS * (t + 1))
                if t >= 1:
                    pe.wait_ge(xatt["probs_t"], t)
                for n in range(XHEADS * NM):
                    h, m = divmod(n, NM)
                    mm = pe.transpose(bank(4, 2)[:, n * P:(n + 1) * P], probs[:, t % 2, h, m * P:(m + 1) * P], ident[:, :])
                mm.then_inc(xatt["turned"], 1)

            def mem_values(t):
                pe.wait_ge(xatt["probs_t"], t + 1)
                if t >= 1:
                    pe.wait_ge(xatt["o_full"], t)
                for k in range(NK):
                    h = k // (NK // XHEADS)
                    for m in range(NM):
                        mm = pe.matmul(bank(6, 2)[:, k * P:(k + 1) * P], mem_v[:, m, k * P:(k + 1) * P],
                                       probs_t[:, (h * NM + m) * P:(h * NM + m + 1) * P], start=m == 0, stop=m == NM - 1)
                mm.then_inc(xatt["o"], 1)

            def project_o(t):
                if t == 0:
                    for s in range(2):
                        pe.wait_ge(w_full[s], uses.n[s] + 1)
                pe.wait_ge(xatt["o_full"], t + 1)
                if t >= 2:
                    pe.wait_ge(xo["y"], t - 1)
                for s in range(2):
                    mm = rows_part(pe, 2 + t % 2, t, s, x_hi, x_lo)
                    if s == 0 and t == NT - 1:
                        mm.then_inc(xo["half"], 1)
                mm.then_inc(xo["full"], 1)

            logits(0)
            for t in range(NT):
                if t + 1 < NT:
                    logits(t + 1)
                turn_probs(t)
                mem_values(t)
            for t in range(NT):
                project_o(t)
            for s in range(2):
                uses.n[s] += 1
            x_xo = {"src": (x_hi, x_lo), "half": xo["half"], "full": xo["full"]}

            def xo_wait(t):
                if t in (2, 3):
                    pe.wait_ge(xo["y"], NT + t - 3)
                if t >= 4:
                    pe.wait_ge(xo["y"], NT + t - 3)

            pairs(x_xo, 1, xo_wait, lambda p, n: ahead(norm3, p, n))

            def norm3_turns(n):
                if n in (1, 2):
                    turn(pe, norm3, NT - 3 + n)

            ffn_pe(pe, uses, CHUNKS, norm3["x_full"], lambda: pe.wait_ge(xo["y"], 2 * NT), norm3_turns, nothing)


_INS = ["x", "mem", "ffn1_pre_g", "ffn1_post_g", "ffn1_w_gate", "ffn1_w_up", "ffn1_w_down", "mix_pre_g",
        "mix_post_g", "w_in", "sgu_norm_g", "sgu_norm_b", "sgu_w_s", "sgu_b_s", "sgu_out_g", "sb_out_g", "w_out",
        "xa_pre_g", "xa_post_g", "mem_norm_g", "xa_w_q", "xa_w_kv", "xa_w_o", "ffn2_pre_g", "ffn2_post_g",
        "ffn2_w_gate", "ffn2_w_up", "ffn2_w_down", "final_norm_g"]


def kernel(**inputs):
    import numpy as _np
    import concourse.bacc as _bacc
    from concourse import mybir as _mybir
    from concourse.bass_utils import run_bass_kernel_spmd as _run

    nc = _bacc.Bacc("TRN2", target_bir_lowering=False, num_devices=1)
    arrays, args = {}, {}
    for name in _INS:
        v = _np.ascontiguousarray(inputs[name])
        arrays[f"in_{name}"] = v
        args[name] = nc.dram_tensor(f"in_{name}", v.shape, _mybir.dt.from_np(v.dtype), kind="ExternalInput").ap()
    out = nc.dram_tensor("out_0", inputs["x"].shape, _mybir.dt.float32, kind="ExternalOutput").ap()
    build(nc, args, out)
    r = _run(nc, [arrays], core_ids=[0])
    return r.results[0]["out_0"]
```

```python
from contextlib import ExitStack

import concourse.bass as bass
from concourse import mybir

ACT = mybir.ActivationFunctionType
ALU = mybir.AluOpType
AX = mybir.AxisListType
F32 = mybir.dt.float32
F32R = mybir.dt.float32r
BF16 = mybir.dt.bfloat16

P = 128
BANK = 512
EPS = 1e-6
MASKED = -1e30


class Uses:

    def __init__(self):
        self.n = [0, 0, 0]


def build(nc, a, out):
    S, D = a["x"].shape[1:]
    M = a["mem"].shape[1]
    FF = a["ffn1_w_gate"].shape[2]
    G, CH = a["sgu_w_s"].shape[1:3]
    SW = a["sgu_out_g"].shape[1]
    GD = SW // G
    SBW = a["sb_out_g"].shape[1]
    HD = 64
    SBH = SBW // HD
    XHEADS = 4
    XHD = D // XHEADS
    NT = S // P
    NK = D // P
    NM = M // P
    NF = FF // P
    CHUNKS = NF // 2
    PAIRS = NT // 2
    SLOT = 2 * D
    HALF = S // 2
    COLS = 256
    QK_BLOCKS = 2 * SBW // COLS
    XK_BLOCKS = D // COLS
    N_ATT = NT * SBH
    PAIR_STEPS = 2 * SBH

    def att_step(n):
        p, r = divmod(n, PAIR_STEPS)
        h, short = divmod(r, 2)
        return (p if short else NT - 1 - p), h

    ATT_ORDER = [i for p in range(NT // 2) for i in (NT - 1 - p, p)]
    ATT_PLACE = [ATT_ORDER.index(i) for i in range(NT)]
    U_COLS, VG_COLS, Q_COLS = 0, SW, 2 * SW
    V_COLS = 2 * SW + 2 * SBW
    assert S == D == 1024 and NF % 2 == 0 and CH == P and GD == P and HALF == BANK == SW == SBW and NM == 2

    ctx = ExitStack()
    with ctx:
        def sem(name):
            return ctx.enter_context(nc.semaphore(name))

        def sems(stage, *names):
            return {n: sem(f"{stage}_{n}") for n in names}

        def sb(name, shape, dt=F32):
            return ctx.enter_context(nc.sbuf_tensor(name, shape, dt))

        def overlay(*tensors):
            with ExitStack() as place:
                return [place.enter_context(nc.sbuf_tensor(n, shape, dt)) for n, shape, dt in tensors]

        w_raw = sb("w_raw", [P, 2, SLOT])
        w_hi = sb("w_hi", [P, 2, SLOT], F32R)
        w_lo = sb("w_lo", [P, 2, SLOT], F32R)
        resid_a, vg = overlay(("resid_a", [P, 2, D], F32), ("vg", [P, NT, SW], F32))
        mem_v, o_left = overlay(("mem_v", [P, NM, D], F32), ("o_left", [P, NT, BANK], F32))
        q_odd, = overlay(("q_odd", [P, SBW // P, S], F32))
        w2_raw = sb("w2_raw", [P, SLOT])
        w2_hi = sb("w2_hi", [P, SLOT], F32R)
        w2_lo = sb("w2_lo", [P, SLOT], F32R)
        m_hi = w2_hi[:, :].rearrange("p (k m) -> p k m", m=M)
        m_lo = w2_lo[:, :].rearrange("p (k m) -> p k m", m=M)

        ident = sb("ident", [P, P])
        ident_bf = sb("ident_bf", [P, P], BF16)
        causal_neg = sb("causal_neg", [P, P], BF16)
        ws_t, = overlay(("ws_t", [P, G, P], F32))
        square_out = sb("square_out", [P, D], BF16)
        last_act, last_product = overlay(("last_act", [P, HALF], F32), ("last_product", [P, HALF], F32))
        sgu_bc = sb("sgu_bc", [P, 2, SW])
        sums = sb("sums", [P, 2 * NT])
        rstd = sb("rstd", [P, 2 * NT])
        half_pow = sb("half_pow", [P, 8])
        small = sb("small", [P, 96])

        beta, keep, suffix, attn_t = overlay(
            ("beta", [P, 3, S], F32), ("keep", [P, 2, S], F32), ("suffix", [P, 2, S + 8], F32),
            ("attn_t", [P, 2, S], F32))
        x_hi = sb("x_hi", [P, NK, S], F32R)
        x_lo = sb("x_lo", [P, NK, S], F32R)

        u_sb, q_even, v_sb, k_t = overlay(
            ("u_sb", [P, NT, SW], F32), ("q_even", [P, SBW // P, S], F32), ("v_sb", [P, NT, SBW], F32),
            ("k_t", [P, SBW // P, S], F32))
        out_b = q_even
        xq_t, resid_b, mem_k, probs, probs_t = overlay(
            ("xq_t", [P, NK, S], F32), ("resid_b", [P, 2, D], F32), ("mem_k", [P, NK, M], F32),
            ("probs", [P, 2, XHEADS, M], F32), ("probs_t", [P, D], F32))
        y = sb("y", [P, NT, D])
        ws_raw, = overlay(("ws_raw", [P, G, P], F32))
        hid_hi = sb("hid_hi", [P, 2, S], F32R)
        hid_lo = sb("hid_lo", [P, 2, S], F32R)
        normed, = overlay(("normed", [P, 2, D], F32))
        gate_act = sb("gate_act", [P, 2, HALF])
        product = sb("product", [P, 2, HALF])
        gain_post = sb("gain_post", [P, D])
        gain_pre = sb("gain_pre", [P, D])

        def gate_tile(q, last):
            return last_act[:, :] if last and q == 3 else gate_act[:, q % 2, :]

        def product_tile(q, last):
            return last_product[:, :] if last and q == 3 else product[:, q % 2, :]

        def raw(s):
            return w_raw[:, s, :] if s < 2 else w2_raw[:, :]

        def hi(s):
            return w_hi[:, s, :] if s < 2 else w2_hi[:, :]

        def lo(s):
            return w_lo[:, s, :] if s < 2 else w2_lo[:, :]

        ps = ctx.enter_context(nc.psum_tensor("ps", [P, 8, BANK], F32))

        def bank(b, n=1):
            return ps[:, b:b + n, :].rearrange("p b c -> p (b c)")

        def turn_bank(t):
            return bank(4 + 2 * (t % 2), 2)

        h_dram = [nc.dram_tensor(f"h_scratch{i}", [S, D], F32, kind="Internal").ap() for i in range(3)]
        x_in = a["x"][0]

        raw_full = [sem(f"raw_full{s}") for s in range(3)]
        hi_done = [sem(f"hi_done{s}") for s in range(3)]
        w_full = [sem(f"w_full{s}") for s in range(3)]
        own_result = sem("own_result")

        PRE = ("gains", "sum_h", "rstd_h", "normed")
        POST = ("sum_y", "rstd_y", "scaled", "h", "stored0", "stored1")
        TURN = ("turned", "x_hi", "x_full")
        norm0 = sems("norm0", *PRE, *TURN)
        norm1 = sems("norm1", *POST, *PRE, *TURN)
        merge = sems("merge", *PRE, *TURN, "sum_y", "rstd_y", "left")
        norm2 = sems("norm2", *POST, *PRE, *TURN)
        norm3 = sems("norm3", *POST, *PRE, *TURN)
        norm4 = sems("norm4", "gains", "sum_y", "rstd_y", "scaled", "h", "sum_h", "rstd_h", "unit", "normed",
                     "last_normed")
        norm_mem = sems("norm_mem", *PRE, *TURN)
        x_tile = [sem(f"x_tile{t}") for t in range(NT)]
        resid_full = [sem(f"resid_full{u}") for u in range(2)]
        norm1["loads"], norm_mem["loads"], norm2["loads"] = 0, NT // 2, (NT + NM) // 2
        norm3["loads"], norm4["loads"] = (2 * NT + NM) // 2, (3 * NT + NM) // 2

        ffn = sems("ffn", "gu", "gate_act", "product", "hid_hi", "hid_full", "down", "y")
        mix = sems("mix", "half", "full", "u", "vg", "bn", "stats", "rstd", "centred", "gained", "vn", "mixed",
                   "out_a", "qk", "qk_done", "const", "ws_raw", "masked", "ws_turned", "ws", "v_done", "padded")
        sb_att = sems("sb", "ones", "z", "beta", "keep", "suffix", "attn", "turned", "attn_t", "av", "out_b")
        wout = sems("wout", "half", "full", "y")
        xkv = sems("xkv", "k", "k_done", "half", "v", "v_done")
        xq = sems("xq", "q", "q_done")
        xatt = sems("xatt", "logits", "max", "neg", "probs", "recip", "scaled", "turned", "probs_t", "o", "o_hi",
                    "o_full")
        xo = sems("xo", "half", "full", "y", "left")
        stored_out = sem("stored_out")

        block = ctx.enter_context(nc.Block())

        def load_block(sp, uses, s, halves, ahead=0):
            n = uses.n[s]
            if n or not isinstance(ahead, int):
                sp.wait_ge(w_full[s], n + ahead)
            for dst, src in halves:
                sp.dma_start(dst, src).then_inc(raw_full[s], 16)

        def block_cols(name, s, c0):
            w = a[name][0].rearrange("(k p) c -> p k c", p=P)
            dst = raw(s).rearrange("p (k c) -> p k c", c=COLS)
            h = NK // 2
            return [(dst[:, i * h:(i + 1) * h, :], w[:, i * h:(i + 1) * h, c0:c0 + COLS]) for i in range(2)]

        def block_rows(name, s, k0, c0):
            w = a[name][0].rearrange("(k p) c -> p k c", p=P)
            dst = raw(s).rearrange("p (k c) -> p k c", c=BANK)
            return [(dst[:, 2 * i:2 * i + 2, :], w[:, k0 + 2 * i:k0 + 2 * i + 2, c0:c0 + BANK]) for i in range(2)]

        def gate_up(p, f, tile):
            dst = raw(f).rearrange("p (g k c) -> p g k c", g=2, c=P)
            gate = a[p + "_w_gate"][0].rearrange("(k p) c -> p k c", p=P)
            up = a[p + "_w_up"][0].rearrange("(k p) c -> p k c", p=P)
            return [(dst[:, 0], gate[:, :, bass.ds(tile * P, P)]), (dst[:, 1], up[:, :, bass.ds(tile * P, P)])]

        def down_rows(p, chunk):
            w = a[p + "_w_down"][0].rearrange("(f p) c -> p f c", p=P)
            return [(w2_raw[:, f * D:(f + 1) * D], w[:, bass.ds(2 * chunk + f, 1), :].rearrange("p f c -> p (f c)"))
                    for f in range(2)]

        def logits_bank(t):
            return bank(2 if t == 1 else 0, 2)

        def last_bank(c0, n):
            if n < 6:
                return 4 + n % 4
            return (n - 6) % (4 if c0 == 0 else 8)

        @block.sync
        def _(sp):
            uses = Uses()

            def one(s, halves):
                load_block(sp, uses, s, halves)
                uses.n[s] += 1

            def rows(name, c0):
                for s in range(2):
                    one(s, block_rows(name, s, 4 * s, c0))

            def ffn_rest(p):
                one(2, down_rows(p, 0))
                with sp.Fori(1, CHUNKS) as i:
                    for f in range(2):
                        load_block(sp, uses, f, gate_up(p, f, 2 * i + f), i - 1)
                    load_block(sp, uses, 2, down_rows(p, i), i - 1)
                for s in range(3):
                    uses.n[s] += CHUNKS - 1

            def x_tiles(t0, t1):
                for t in range(t0, t1):
                    sp.dma_start(y[:, t, :], x_in[t * P:(t + 1) * P, :]).then_inc(x_tile[t], 16)

            x_tiles(0, 2)
            sp.dma_start(gain_pre[:, :], a["ffn1_pre_g"].broadcast_to((P, D))).then_inc(norm0["gains"], 16)
            x_tiles(2, 4)
            one(0, gate_up("ffn1", 0, 0))
            x_tiles(4, 6)
            one(1, gate_up("ffn1", 1, 1))
            x_tiles(6, NT)
            ffn_rest("ffn1")
            rows("w_in", U_COLS)
            sp.wait_ge(ffn["down"], 2 * NT * CHUNKS)
            sp.dma_start(sgu_bc[:, 0, :], a["sgu_norm_g"][0].rearrange("(o g) d -> o (g d)", o=1)
                         .broadcast_to((P, SW))).then_inc(mix["const"], 16)
            sp.dma_start(sgu_bc[:, 1, :], a["sgu_norm_b"][0].rearrange("(o g) d -> o (g d)", o=1)
                         .broadcast_to((P, SW))).then_inc(mix["const"], 16)
            sp.dma_start(small[:, 0:G], a["sgu_b_s"][0].rearrange("g t -> t g"),
                         allow_slow_non_contiguous=True).then_inc(mix["const"], 16)
            sp.dma_start(ws_raw[:, :, :], a["sgu_w_s"][0].rearrange("g t s -> t g s")).then_inc(mix["ws_raw"], 16)
            rows("w_in", VG_COLS)
            rows("w_in", V_COLS)
            for b in range(QK_BLOCKS):
                one(b % 2, block_cols("w_in", b % 2, Q_COLS + b * COLS))
            for cb in range(2):
                rows("w_out", cb * BANK)
            for b in range(XK_BLOCKS):
                one(b % 2, block_cols("xa_w_kv", b % 2, b * COLS))
            for cb in range(2):
                rows("xa_w_kv", D + cb * BANK)
            for b in range(XK_BLOCKS):
                one(b % 2, block_cols("xa_w_q", b % 2, b * COLS))
            for cb in range(2):
                rows("xa_w_o", cb * BANK)
            for f in range(2):
                one(f, gate_up("ffn2", f, f))
            sp.wait_ge(xatt["o"], NT)
            ffn_rest("ffn2")
            for t in range(NT):
                if t < NT - 2:
                    sp.wait_ge(norm4["normed"], t + 1)
                else:
                    sp.wait_ge(norm4["last_normed"], t - NT + 3)
                sp.dma_start(out[0, t * P:(t + 1) * P, :], y[:, t, :]).then_inc(stored_out, 16)
            sp.wait_ge(stored_out, 16 * NT)

        CONSTANT_STEPS = 7
        own = [CONSTANT_STEPS]

        def after(pool, op):
            own[0] += 1
            op.then_inc(own_result, 1)
            pool.wait_ge(own_result, own[0])

        def rstd_y(pool, s, t, width=D, n=None):
            pool.wait_ge(s["sum_y"], (t if n is None else n) + 1)
            after(pool, pool.tensor_scalar(sums[:, t:t + 1], sums[:, t:t + 1], 1.0 / width, EPS, ALU.mult, ALU.add))
            pool.tensor_tensor(rstd[:, t:t + 1], sums[:, t:t + 1], half_pow[:, 0:1], ALU.pow).then_inc(s["rstd_y"], 1)

        def rstd_h(pool, s, t, width=D, n=None):
            col = slice(NT + t, NT + t + 1)
            pool.wait_ge(s["sum_h"], (t if n is None else n) + 1)
            after(pool, pool.tensor_scalar(sums[:, col], sums[:, col], 1.0 / width, EPS, ALU.mult, ALU.add))
            pool.tensor_tensor(rstd[:, col], sums[:, col], half_pow[:, 0:1], ALU.pow).then_inc(s["rstd_h"], 1)

        @block.gpsimd
        def _(pool):
            pool.memset(half_pow[:, :], -0.5).then_inc(own_result, 1)
            pool.memset(ident[:, :], 0.0).then_inc(own_result, 1)
            pool.memset(ident_bf[:, :], 0.0).then_inc(own_result, 1)
            pool.memset(causal_neg[:, :], 0.0).then_inc(own_result, 1)
            pool.wait_ge(own_result, 4)
            for m in (ident, ident_bf):
                pool.affine_select(out=m[:, :], in_=m[:, :], compare_op=ALU.not_equal, fill=1.0, base=0,
                                   pattern=[[-1, P]], channel_multiplier=1).then_inc(own_result, 1)
            pool.affine_select(out=causal_neg[:, :], in_=causal_neg[:, :], compare_op=ALU.is_gt, fill=MASKED,
                               base=0, pattern=[[-1, P]], channel_multiplier=1).then_inc(own_result, 1)
            for t in range(NT):
                rstd_h(pool, norm0, t)

            def norm_pairs(s):
                for p in range(PAIRS):
                    for t in (2 * p, 2 * p + 1):
                        rstd_y(pool, s, t)
                    for t in (2 * p, 2 * p + 1):
                        rstd_h(pool, s, t)

            def norm_tiles(s, finish=lambda t: None):
                rstd_y(pool, s, 0)
                for t in range(1, NT + 1):
                    if t == 3:
                        rstd_h(pool, s, 2)
                    if t < NT:
                        rstd_y(pool, s, t)
                    if t != 3:
                        rstd_h(pool, s, t - 1)
                    if t >= 2:
                        finish(t - 2)

            norm_tiles(norm1)
            pool.wait_ge(mix["ws_raw"], 16)
            pool.affine_select(out=ws_raw[:, :, :], in_=ws_raw[:, :, :], compare_op=ALU.is_ge, fill=0.0, base=0,
                               pattern=[[0, G], [-1, P]], channel_multiplier=1).then_inc(mix["masked"], 1)
            for t in range(NT):
                pool.wait_ge(mix["stats"], G * (t + 1))
                var = small[:, 32 + 8 * (t % 2):40 + 8 * (t % 2)].rearrange("p (g two) -> p g two", two=2)[:, :, 1]
                after(pool, pool.tensor_scalar(var, var, 1.0, EPS, ALU.mult, ALU.add))
                pool.tensor_tensor(var, var, half_pow[:, 0:G], ALU.pow).then_inc(mix["rstd"], 1)
            pool.wait_ge(norm1["stored1"], 16 * PAIRS)
            pool.wait_ge(norm1["normed"], NT)
            pool.wait_ge(mix["rstd"], NT)
            pool.memset(q_even[HD:P, :, :], 0.0).then_inc(mix["padded"], 1)
            pool.wait_ge(mix["mixed"], NT)
            pool.wait_ge(mix["padded"], 1)
            pool.memset(q_odd[0:HD, :, :], 0.0).then_inc(mix["padded"], 1)
            pool.wait_ge(mix["padded"], 2)
            for n, t in enumerate(ATT_ORDER):
                rstd_y(pool, merge, t, SW, n)
                rstd_h(pool, merge, t, SBW, n)
            for t in range(NM):
                rstd_h(pool, norm_mem, t)
            norm_pairs(norm2)
            pool.wait_ge(xatt["logits"], NT)
            for t in range(NT):
                pool.wait_ge(xo["y"], t + 1)
                pool.tensor_copy(y[:, t, 0:BANK], o_left[:, t, :]).then_inc(xo["left"], 1)
            norm_pairs(norm3)

            def gain(t):
                if t < NT - 2:
                    pool.wait_ge(norm4["unit"], t + 1)
                    pool.tensor_tensor(y[:, t, :], y[:, t, :], gain_pre[:, :], ALU.mult).then_inc(norm4["normed"], 1)

            norm_tiles(norm4, gain)

        def split_hi(act, s, n):
            act.wait_ge(raw_full[s], n * 32)
            act.activation(hi(s), raw(s), ACT.Copy).then_inc(hi_done[s], 1)

        def next_hi(act, uses, s, ready, n):
            act.wait_ge(ready, n)
            uses.n[s] += 1
            split_hi(act, s, uses.n[s])

        def load_resid(act, s, place, src, t):
            act.dma_start(place[:, t % 2, :], src[t * P:(t + 1) * P, :]).then_inc(resid_full[t % 2], 16)

        def wait_resid(eng, s, t):
            eng.wait_ge(resid_full[t % 2], 16 * (s["loads"] + t // 2 + 1))

        def load_gains(act, s, post, pre):
            if post is not None:
                act.dma_start(gain_post[:, :], a[post].broadcast_to((P, D))).then_inc(s["gains"], 16)
            act.dma_start(gain_pre[:, :], a[pre].broadcast_to((P, D))).then_inc(s["gains"], 16)

        def ffn_act(act, uses, c0, last_part):
            def hidden(i, q, first, last=False):
                f, h = q % 2, q // 2
                idx = 4 * i + q
                act.wait_ge(ffn["gu"], 2 * idx + 1)
                if not (first and q < 2):
                    act.wait_ge(ffn["product"], idx - 1)
                act.activation(gate_tile(q, last), bank(2 * (q % 2)), ACT.Silu).then_inc(ffn["gate_act"], 1)
                act.wait_ge(ffn["product"], idx + 1)
                if not first:
                    act.wait_ge(ffn["down"], 2 * NT * i)
                act.activation(hid_hi[:, f, h * HALF:(h + 1) * HALF], product_tile(q, last), ACT.Copy)\
                   .then_inc(ffn["hid_hi"], 1)

            def chunk(i, first, last):
                hidden(i, 0, first)
                if not first:
                    act.wait_ge(ffn["down"], 2 * NT * i)
                split_hi(act, 2, i + 1)
                hidden(i, 1, first)
                hidden(i, 2, first)
                if last:
                    uses.n[2] += 1
                    last_part(lambda: hidden(i, 3, first, True))
                    return
                act.wait_ge(ffn["gu"], 8 * i + 6)
                split_hi(act, 0, uses.n[0] + 1 - c0 + i)
                hidden(i, 3, first)
                act.wait_ge(ffn["gu"], 8 * i + 8)
                split_hi(act, 1, uses.n[1] + 1 - c0 + i)

            chunk(c0, True, False)
            with act.Fori(c0 + 1, c0 + CHUNKS - 1) as i:
                chunk(i, False, False)
            for f in range(3):
                uses.n[f] += CHUNKS - 1
            chunk(c0 + CHUNKS - 1, False, True)

        @block.scalar
        def _(act):
            uses = Uses()
            last_square = []

            def square_sum(src, col, done, n, width=D, parts=None):
                if last_square:
                    act.wait_ge(*last_square[-1])
                dst = square_out[:, 0:width]
                if parts:
                    dst = dst.rearrange("p (c d) -> p c d", d=parts)
                act.activation(dst, src, ACT.Square, accum_out=sums[:, col:col + 1]).then_inc(done, 1)
                last_square.append((done, n))

            def square_y(s, t):
                square_sum(y[:, t, :], t, s["sum_y"], t + 1)

            def square_h(s, t, store, place, src):
                act.wait_ge(s["h"], t + 1)
                square_sum(y[:, t, :], NT + t, s["sum_h"], t + 1)
                if store is not None:
                    act.dma_start(store[t * P:(t + 1) * P, :], y[:, t, :]).then_inc(s[f"stored{t // PAIRS}"], 16)
                if t + 2 < NT:
                    load_resid(act, s, place, src, t + 2)

            def turn_hi(s, t, dst):
                act.wait_ge(s["turned"], t + 1)
                act.activation(dst[:, :, t * P:(t + 1) * P], turn_bank(t).rearrange("p (k c) -> p k c", c=P),
                               ACT.Copy).then_inc(s["x_hi"], 1)

            def project_y(s, cb, t):
                act.wait_ge(s["full"], cb * NT + t + 1)
                act.activation(y[:, t, cb * BANK:(cb + 1) * BANK], bank(t % 4), ACT.Copy).then_inc(s["y"], 1)

            def project_and_norm(uses, st, s, store, src, between=lambda: None):
                def pair(p):
                    return (2 * p, 2 * p + 1)

                for p in range(PAIRS):
                    last = p == PAIRS - 1
                    if last:
                        next_hi(act, uses, 0, st["half"], 2)
                    for t in pair(p):
                        project_y(st, 1, t)
                    if last:
                        for t in pair(p - 1):
                            turn_hi(s, t, x_hi)
                        next_hi(act, uses, 1, st["full"], 2 * NT)
                    for t in pair(p):
                        act.wait_ge(st["y"], NT + t + 1)
                        if st is xo:
                            act.wait_ge(xo["left"], t + 1)
                        square_y(s, t)
                    if last:
                        between()
                    for t in pair(p):
                        square_h(s, t, store, resid_b, src)
                    if p < PAIRS - 2:
                        for t in pair(p):
                            turn_hi(s, t, x_hi)

            def x_squares(t0, t1):
                for t in range(t0, t1):
                    act.wait_ge(x_tile[t], 16)
                    square_sum(y[:, t, :], NT + t, norm0["sum_h"], t + 1)

            def x_turned(t0, t1):
                for t in range(t0, t1):
                    turn_hi(norm0, t, x_hi)

            def first_hi(s):
                uses.n[s] += 1
                split_hi(act, s, 1)

            x_squares(0, 4)
            x_turned(0, 2)
            first_hi(0)
            x_turned(2, 4)
            x_squares(4, 6)
            first_hi(1)
            x_squares(6, NT)
            x_turned(4, NT)
            load_gains(act, norm1, "ffn1_post_g", "mix_pre_g")
            def first_residuals(s, src, n):
                act.wait_ge(w_full[2], n)
                for t in range(2):
                    load_resid(act, s, resid_a, src, t)

            def u_tile(t):
                act.wait_ge(mix["full"], t + 1)
                if t == 0:
                    act.wait_ge(norm1["stored0"], 16 * PAIRS)
                act.activation(u_sb[:, t, :], bank(t % 4), ACT.Gelu_apprx_tanh).then_inc(mix["u"], 1)

            def last_sums(s, c0, t):
                act.wait_ge(ffn["y"], 2 * NT * (c0 + CHUNKS - 1) + 2 * t + 2)
                square_y(s, t)

            def ffn1_end(hidden3):
                def h(t):
                    square_h(norm1, t, h_dram[0], resid_a, x_in)

                def turned(t):
                    if t == 4:
                        act.wait_ge(ffn["gu"], 8 * CHUNKS)
                    turn_hi(norm1, t, x_hi)

                first_residuals(norm1, x_in, CHUNKS)
                next_hi(act, uses, 0, ffn["gu"], 8 * CHUNKS - 2)
                last_sums(norm1, 0, 0)
                last_sums(norm1, 0, 1)
                h(0)
                last_sums(norm1, 0, 2)
                h(1)
                hidden3()
                turned(0)
                h(2)
                next_hi(act, uses, 1, ffn["gu"], 8 * CHUNKS)
                turned(1)
                for t in range(3, NT + 2):
                    if t < NT:
                        last_sums(norm1, 0, t)
                    if 4 <= t <= NT:
                        h(t - 1)
                    if t >= 4:
                        turned(t - 2)
                    if t >= NT - 1:
                        u_tile(t - NT + 1)

            ffn_act(act, uses, 0, ffn1_end)
            for t in range(3, NT):
                if t == NT - 2:
                    next_hi(act, uses, 0, mix["half"], 1)
                u_tile(t)
            next_hi(act, uses, 1, mix["full"], NT)
            act.wait_ge(mix["ws_turned"], 1)
            act.activation(ws_t[:, :, :], bank(6).rearrange("p (g t) -> p g t", g=G), ACT.Copy).then_inc(mix["ws"], 1)
            for t in range(NT):
                if t == NT - 2:
                    next_hi(act, uses, 0, mix["half"], 2)
                act.wait_ge(mix["full"], NT + t + 1)
                act.activation(vg[:, t, :], bank(t % 4), ACT.Gelu_apprx_tanh).then_inc(mix["vg"], 1)
            next_hi(act, uses, 1, mix["full"], 2 * NT)
            for t in range(NT):
                if t == NT - 2:
                    next_hi(act, uses, 0, mix["half"], 3)
                act.wait_ge(mix["full"], 2 * NT + t + 1)
                act.activation(v_sb[:, t, :], bank(t % 4), ACT.Copy).then_inc(mix["v_done"], 1)
            next_hi(act, uses, 1, mix["full"], 3 * NT)
            act.wait_ge(norm1["stored1"], 16 * PAIRS)
            act.wait_ge(mix["mixed"], NT)
            for b in range(QK_BLOCKS):
                for n in range(4):
                    idx = 4 * b + n
                    tile, h = idx // 2, idx % 2
                    at = slice(h * HALF, (h + 1) * HALF)
                    act.wait_ge(mix["qk"], idx + 1)
                    if b < QK_BLOCKS // 2:
                        for dst, rows in ((q_even, slice(0, HD)), (q_odd, slice(HD, P))):
                            act.activation(dst[rows, tile, at], bank(idx % 4)[rows, :], ACT.Copy, scale=HD ** -0.5)\
                               .then_inc(mix["qk_done"], 1)
                    else:
                        act.activation(k_t[:, tile - SBW // P, at], bank(idx % 4), ACT.Copy).then_inc(mix["qk_done"], 2)
                if b < QK_BLOCKS - 1:
                    next_hi(act, uses, b % 2, mix["qk"], 4 * b + 4)

            def merge_squares(n):
                t = ATT_ORDER[n]
                act.wait_ge(mix["out_a"], G * (t + 1))
                square_sum(u_sb[:, t, :], t, merge["sum_y"], n + 1, SW)
                act.wait_ge(sb_att["out_b"], n + 1)
                square_sum(out_b[:, :, t * P:(t + 1) * P], NT + t, merge["sum_h"], n + 1, SBW, P)

            for n in range(N_ATT + 3):
                if n < N_ATT:
                    u, W = n % 2, (att_step(n)[0] + 1) * P
                    z = bank(2 * u, 2)[:, 0:W]
                    act.wait_ge(sb_att["z"], n + 1)
                    if n >= 3:
                        act.wait_ge(sb_att["turned"], n - 2)
                    act.activation(beta[:, n % 3, 0:W], z, ACT.Sigmoid).then_inc(sb_att["beta"], 1)
                    if n >= 2:
                        act.wait_ge(sb_att["suffix"], n - 1)
                    act.activation(keep[:, u, 0:W], z, ACT.Sigmoid, scale=-1.0).then_inc(sb_att["keep"], 1)
                m = n - 3
                if m >= 0 and m % 2 == 0:
                    W = (att_step(m)[0] + 1) * P
                    act.wait_ge(sb_att["turned"], m + 1)
                    if m >= 2:
                        act.wait_ge(sb_att["av"], m - 1)
                    act.activation(attn_t[:, m % 2, 0:W], bank(4, 2)[:, 0:W], ACT.Copy).then_inc(sb_att["attn_t"], 1)
                if n == 4:
                    next_hi(act, uses, 1, mix["qk"], 4 * QK_BLOCKS)
                if n == N_ATT - 1:
                    act.dma_start(gain_pre[:, 0:SW], a["sgu_out_g"].broadcast_to((P, SW))).then_inc(merge["gains"], 16)
                    act.dma_start(gain_pre[:, SW:D], a["sb_out_g"].broadcast_to((P, SBW))).then_inc(merge["gains"], 16)
                    act.dma_start(gain_post[:, :], a["mem_norm_g"].broadcast_to((P, D))).then_inc(norm_mem["gains"], 16)
                p, r = divmod(n, PAIR_STEPS)
                if p >= 1 and r in (5, 7) and n < N_ATT:
                    merge_squares(2 * p - 2 + (r == 7))
            act.wait_ge(sb_att["av"], N_ATT)
            for t in range(NM):
                load_resid(act, norm_mem, resid_b, a["mem"][0], t)

            for t in range(NT):
                turn_hi(merge, t, x_hi)
                if t == 1:
                    merge_squares(NT - 2)
                    merge_squares(NT - 1)
            for t in range(NM):
                wait_resid(act, norm_mem, t)
                square_sum(resid_b[:, t, :], NT + t, norm_mem["sum_h"], t + 1)
            for t in range(NT):
                if t == NT - 2:
                    next_hi(act, uses, 0, wout["half"], 1)
                project_y(wout, 0, t)
            next_hi(act, uses, 1, wout["full"], NT)
            for t in range(NM):
                turn_hi(norm_mem, t, m_hi)
            act.wait_ge(norm_mem["normed"], NM)
            load_gains(act, norm2, "mix_post_g", "xa_pre_g")
            act.wait_ge(norm1["stored0"], 16 * PAIRS)
            for t in range(2):
                load_resid(act, norm2, resid_b, h_dram[0], t)

            def mem_k_block(b):
                for c in range(2):
                    act.wait_ge(xkv["k"], 2 * b + c + 1)
                    act.activation(mem_k[:, 2 * b + c, :], bank((2 * b + c) % 4)[:, 0:M], ACT.Copy)\
                       .then_inc(xkv["k_done"], 1)
                next_hi(act, uses, b % 2, xkv["k"], 2 * b + 2)

            project_and_norm(uses, wout, norm2, h_dram[1], h_dram[0], lambda: mem_k_block(0))
            mem_k_block(1)
            for t in (NT - 2, NT - 1):
                turn_hi(norm2, t, x_hi)
            for b in range(2, XK_BLOCKS):
                mem_k_block(b)
            for cb in range(2):
                next_hi(act, uses, 0, xkv["half"], cb + 1)
                for t in range(NM):
                    act.wait_ge(xkv["v"], cb * NM + t + 1)
                    act.activation(mem_v[:, t, cb * BANK:(cb + 1) * BANK], bank(2 * cb + t), ACT.Copy)\
                       .then_inc(xkv["v_done"], 1)
                next_hi(act, uses, 1, xkv["v"], (cb + 1) * NM)
            for u in range(2):
                act.wait_ge(norm2[f"stored{u}"], 16 * PAIRS)
            for b in range(XK_BLOCKS):
                for n in range(4):
                    idx = 4 * b + n
                    tile, h = idx // 2, idx % 2
                    act.wait_ge(xq["q"], idx + 1)
                    act.activation(xq_t[:, tile, h * HALF:(h + 1) * HALF], bank(idx % 4), ACT.Copy).then_inc(xq["q_done"], 1)
                if b < XK_BLOCKS - 1:
                    next_hi(act, uses, b % 2, xq["q"], 4 * b + 4)
            for t in range(2):
                load_resid(act, norm3, resid_b, h_dram[1], t)

            def o_hi(t):
                act.wait_ge(xatt["o"], t + 1)
                act.activation(x_hi[:, :, t * P:(t + 1) * P], bank(6, 2).rearrange("p (k c) -> p k c", c=P),
                               ACT.Copy).then_inc(xatt["o_hi"], 1)

            def o_projected(t):
                act.wait_ge(xo["full"], t + 1)
                act.activation(o_left[:, t, :], bank(2 + t % 2), ACT.Copy).then_inc(xo["y"], 1)

            for t in range(NT):
                u = t % 2
                act.wait_ge(xatt["neg"], t + 1)
                if t >= 2:
                    act.wait_ge(xatt["turned"], t - 1)
                for h in range(XHEADS):
                    act.activation(probs[:, u, h, :], logits_bank(t)[:, h * M:(h + 1) * M], ACT.Exp,
                                   bias=small[:, 48 + 4 * u + h:49 + 4 * u + h], scale=XHD ** -0.5,
                                   accum_out=small[:, 56 + 4 * u + h:57 + 4 * u + h]).then_inc(xatt["probs"], 1)
                if t >= 3:
                    o_projected(t - 3)
                if t >= 1:
                    o_hi(t - 1)
                if t == 1:
                    next_hi(act, uses, 1, xq["q"], 4 * XK_BLOCKS)
            o_projected(NT - 3)
            o_hi(NT - 1)
            load_gains(act, norm3, "xa_post_g", "ffn2_pre_g")
            next_hi(act, uses, 0, xo["half"], 1)
            o_projected(NT - 2)
            o_projected(NT - 1)
            next_hi(act, uses, 1, xo["full"], NT)
            project_and_norm(uses, xo, norm3, h_dram[2], h_dram[1])
            for t in (NT - 2, NT - 1):
                turn_hi(norm3, t, x_hi)
            load_gains(act, norm4, "ffn2_post_g", "final_norm_g")

            def ffn2_end(hidden3):
                def h(t):
                    square_h(norm4, t, None, resid_a, h_dram[2])

                def unit(t):
                    act.wait_ge(norm4["rstd_h"], t + 1)
                    act.activation(y[:, t, :], y[:, t, :], ACT.Copy, scale=rstd[:, NT + t:NT + t + 1])\
                       .then_inc(norm4["unit"], 1)

                first_residuals(norm4, h_dram[2], 2 * CHUNKS)
                last_sums(norm4, CHUNKS, 0)
                last_sums(norm4, CHUNKS, 1)
                h(0)
                last_sums(norm4, CHUNKS, 2)
                h(1)
                hidden3()
                h(2)
                unit(0)
                for t in range(3, NT + 1):
                    if t < NT:
                        last_sums(norm4, CHUNKS, t)
                    if t > 3:
                        h(t - 1)
                    if t - 2 < NT - 2:
                        unit(t - 2)

            ffn_act(act, uses, CHUNKS, ffn2_end)

        def split_lo(dve, s, n):
            dve.wait_ge(hi_done[s], n)
            dve.tensor_tensor(lo(s), raw(s), hi(s).bitcast(F32), ALU.subtract).then_inc(w_full[s], 1)

        def next_lo(dve, uses, s):
            uses.n[s] += 1
            split_lo(dve, s, uses.n[s])

        def post_norm(dve, s, t, c, place):
            if t == 0:
                dve.wait_ge(s["gains"], 32)
            dve.wait_ge(s["rstd_y"], t + 1)
            dve.scalar_tensor_tensor(y[:, t, :], y[:, t, :], rstd[:, t:t + 1], gain_post[:, :], ALU.mult, ALU.mult)\
               .then_inc(s["scaled"], 1)
            dve.wait_ge(s["scaled"], t + 1)
            wait_resid(dve, s, t)
            dve.scalar_tensor_tensor(y[:, t, :], y[:, t, :], c, place[:, t % 2, :], ALU.mult, ALU.add)\
               .then_inc(s["h"], 1)

        def pre_norm(dve, s, t, src, gain):
            if t >= 2:
                dve.wait_ge(s["turned"], t - 1)
            dve.wait_ge(s["rstd_h"], t + 1)
            dve.scalar_tensor_tensor(normed[:, t % 2, :], src, rstd[:, NT + t:NT + t + 1], gain, ALU.mult, ALU.mult)\
               .then_inc(s["normed"], 1)

        def turn_lo(dve, s, t, dst_hi, dst_lo):
            dve.wait_ge(s["x_hi"], t + 1)
            at = slice(t * P, (t + 1) * P)
            dve.tensor_tensor(dst_lo[:, :, at], turn_bank(t).rearrange("p (k c) -> p k c", c=P),
                              dst_hi[:, :, at].bitcast(F32), ALU.subtract).then_inc(s["x_full"], 1)

        def norm_and_split(dve, uses, s, split_more):
            for p in range(PAIRS):
                pair = (2 * p, 2 * p + 1)
                early = split_more and p == PAIRS - 1
                for t in pair:
                    post_norm(dve, s, t, 1.0, resid_b)
                    if early and t == pair[0]:
                        next_lo(dve, uses, 0)
                for t in pair:
                    pre_norm(dve, s, t, y[:, t, :], gain_pre[:, :])
                if p == PAIRS - 2:
                    next_lo(dve, uses, 0)
                if early:
                    next_lo(dve, uses, 1)
                for t in pair:
                    turn_lo(dve, s, t, x_hi, x_lo)
                if p == PAIRS - 2:
                    next_lo(dve, uses, 1)

        def ffn_dve(dve, uses, c0, first_y, last_part):
            def hidden(i, q, last=False):
                f, h = q % 2, q // 2
                idx = 4 * i + q
                dve.wait_ge(ffn["gate_act"], idx + 1)
                dve.wait_ge(ffn["gu"], 2 * idx + 2)
                dve.tensor_tensor(product_tile(q, last), gate_tile(q, last), bank(2 * (q % 2) + 1), ALU.mult)\
                   .then_inc(ffn["product"], 1)
                dve.wait_ge(ffn["hid_hi"], idx + 1)
                at = slice(h * HALF, (h + 1) * HALF)
                dve.tensor_tensor(hid_lo[:, f, at], product_tile(q, last), hid_hi[:, f, at].bitcast(F32),
                                  ALU.subtract).then_inc(ffn["hid_full"], 1)

            def chunk(i, first, last):
                hidden(i, 0)
                split_lo(dve, 2, i + 1)
                hidden(i, 1)
                hidden(i, 2)
                if not last:
                    split_lo(dve, 0, uses.n[0] + 1 - c0 + i)
                    hidden(i, 3)
                if first:
                    first_y()
                else:
                    dve.wait_ge(ffn["y"], 2 * NT * i)

                def add(t):
                    for h in range(2):
                        n = 2 * t + h
                        dve.wait_ge(ffn["down"], 2 * NT * i + n + 1)
                        acc = y[:, t, h * BANK:(h + 1) * BANK]
                        if first:
                            op = dve.tensor_copy(acc, bank(4 + n % 4))
                        else:
                            op = dve.tensor_tensor(acc, acc, bank(last_bank(c0, n) if last else 4 + n % 4), ALU.add)
                        op.then_inc(ffn["y"], 1)
                if last:
                    uses.n[2] += 1
                    last_part(lambda: hidden(i, 3, True), add)
                    return
                for t in range(NT):
                    add(t)
                split_lo(dve, 1, uses.n[1] + 1 - c0 + i)

            chunk(c0, True, False)
            with dve.Fori(c0 + 1, c0 + CHUNKS - 1) as i:
                chunk(i, False, False)
            for f in range(3):
                uses.n[f] += CHUNKS - 1
            chunk(c0 + CHUNKS - 1, False, True)

        @block.vector
        def _(dve):
            uses = Uses()
            dve.wait_ge(norm0["gains"], 16)

            def x_normed(t):
                pre_norm(dve, norm0, t, y[:, t, :], gain_pre[:, :])

            def x_turned(t):
                turn_lo(dve, norm0, t, x_hi, x_lo)

            for t in range(4):
                x_normed(t)
                if t >= 2:
                    x_turned(t - 2)
            next_lo(dve, uses, 0)
            x_turned(2)
            x_turned(3)
            x_normed(4)
            x_normed(5)
            next_lo(dve, uses, 1)
            for t in range(4, NT):
                x_turned(t)
                if t + 2 < NT:
                    x_normed(t + 2)

            def ffn1_end(hidden3, add):
                def post(t):
                    post_norm(dve, norm1, t, 0.5, resid_a)

                def pre(t):
                    pre_norm(dve, norm1, t, y[:, t, :], gain_pre[:, :])

                def turned(t):
                    turn_lo(dve, norm1, t, x_hi, x_lo)

                add(0)
                add(1)
                next_lo(dve, uses, 0)
                add(2)
                post(0)
                post(1)
                pre(0)
                post(2)
                pre(1)
                hidden3()
                turned(0)
                add(3)
                turned(1)
                add(4)
                pre(2)
                add(5)
                post(3)
                add(6)
                add(7)
                next_lo(dve, uses, 1)
                turned(2)
                pre(3)
                for t in range(4, NT + 1):
                    if t < NT:
                        post(t)
                    turned(t - 1)
                    if t < NT:
                        pre(t)

            ffn_dve(dve, uses, 0, lambda: None, ffn1_end)
            next_lo(dve, uses, 0)
            next_lo(dve, uses, 1)

            def centre(t):
                stats = small[:, 64:64 + 6 * G].rearrange("p (g six) -> p g six", six=6)
                mean_var = small[:, 32 + 8 * (t % 2):40 + 8 * (t % 2)].rearrange("p (g two) -> p g two", two=2)
                dve.wait_ge(mix["vg"], t + 1)
                if t:
                    dve.wait_ge(mix["stats"], G * t)
                for g in range(G):
                    dve.bn_stats(stats[:, g, :], vg[:, t, g * GD:(g + 1) * GD]).then_inc(mix["bn"], 1)
                if t >= 2:
                    dve.wait_ge(mix["centred"], G * (t - 1))
                for g in range(G):
                    dve.wait_ge(mix["bn"], G * t + g + 1)
                    dve.bn_aggr(mean_var[:, g, :], stats[:, g, :]).then_inc(mix["stats"], 1)

            def gain(t):
                mean_var = small[:, 32 + 8 * (t % 2):40 + 8 * (t % 2)].rearrange("p (g two) -> p g two", two=2)
                if t == 0:
                    dve.wait_ge(mix["const"], 48)
                dve.wait_ge(mix["rstd"], t + 1)
                for g in range(G):
                    at = vg[:, t, g * GD:(g + 1) * GD]
                    dve.tensor_scalar(at, at, mean_var[:, g, 0:1], mean_var[:, g, 1:2], ALU.subtract, ALU.mult)\
                       .then_inc(mix["centred"], 1)
                dve.wait_ge(mix["centred"], G * (t + 1))
                dve.tensor_tensor(vg[:, t, :], vg[:, t, :], sgu_bc[:, 0, :], ALU.mult).then_inc(mix["gained"], 1)
                dve.wait_ge(mix["gained"], t + 1)
                dve.tensor_tensor(vg[:, t, :], vg[:, t, :], sgu_bc[:, 1, :], ALU.add).then_inc(mix["vn"], 1)

            def gate(t):
                dve.wait_ge(mix["mixed"], t + 1)
                for g in range(G):
                    at = slice(g * GD, (g + 1) * GD)
                    dve.scalar_tensor_tensor(u_sb[:, t, at], bank(4 + t % 2)[:, at], small[:, g:g + 1], u_sb[:, t, at],
                                             ALU.add, ALU.mult).then_inc(mix["out_a"], 1)

            for t in range(NT):
                if t == NT - 2:
                    next_lo(dve, uses, 0)
                centre(t)
                if t == NT - 1:
                    next_lo(dve, uses, 1)
                if t >= 1:
                    gain(t - 1)
            gain(NT - 1)
            for t in range(NT):
                gate(t)
                if t == NT - 3:
                    next_lo(dve, uses, 0)
            next_lo(dve, uses, 1)
            for b in range(QK_BLOCKS - 1):
                next_lo(dve, uses, b % 2)

            dve.wait_ge(mix["qk"], 4 * QK_BLOCKS)

            def out_b_tile(n):
                i = ATT_ORDER[n]
                dve.wait_ge(sb_att["av"], PAIR_STEPS * (n // 2 + 1) - 1 + n % 2)
                dve.tensor_copy(out_b[:, :, i * P:(i + 1) * P], bank(6 + i % 2).rearrange("p (c d) -> p c d", d=P))\
                   .then_inc(sb_att["out_b"], 1)

            def copy_turned(m):
                W = (att_step(m)[0] + 1) * P
                dve.wait_ge(sb_att["turned"], m + 1)
                if m >= 2:
                    dve.wait_ge(sb_att["av"], m - 1)
                dve.tensor_copy(attn_t[:, m % 2, 0:W], bank(4, 2)[:, 0:W]).then_inc(sb_att["attn_t"], 1)

            for n in range(N_ATT):
                i, h = att_step(n)
                u, W = n % 2, (i + 1) * P
                m = n - 3
                if m >= 0 and m % 2:
                    copy_turned(m)
                if n >= 2:
                    dve.wait_ge(sb_att["attn"], n - 1)
                if h == 0:
                    dve.memset(suffix[:, u, W:W + 1], 1.0).then_inc(sb_att["ones"], 1)
                dve.wait_ge(sb_att["keep"], n + 1)
                backwards = keep[:, u, 0:W][:, ::-1]
                dve.tensor_tensor_scan(suffix[:, u, 0:W][:, ::-1], backwards, backwards, 1.0, ALU.mult, ALU.bypass)\
                   .then_inc(sb_att["suffix"], 1)
                dve.wait_ge(sb_att["suffix"], n + 1)
                dve.wait_ge(sb_att["ones"], 2 * (n // PAIR_STEPS) + 1 + (n % PAIR_STEPS > 0))
                dve.tensor_tensor(beta[:, n % 3, 0:W], beta[:, n % 3, 0:W], suffix[:, u, 1:W + 1], ALU.mult)\
                   .then_inc(sb_att["attn"], 1)
                if n == 4:
                    next_lo(dve, uses, 1)
                p, r = divmod(n, PAIR_STEPS)
                if p >= 1 and r in (2, 3):
                    out_b_tile(2 * p - 4 + r)

            dve.wait_ge(merge["gains"], 32)

            def merge_tile(t):
                u = t % 2
                if t >= 2:
                    dve.wait_ge(merge["turned"], t - 1)
                dve.wait_ge(merge["rstd_y"], ATT_PLACE[t] + 1)
                dve.scalar_tensor_tensor(normed[:, u, 0:SW], u_sb[:, t, :], rstd[:, t:t + 1], gain_pre[:, 0:SW],
                                         ALU.mult, ALU.mult).then_inc(merge["left"], 1)
                dve.wait_ge(merge["rstd_h"], ATT_PLACE[t] + 1)
                dve.scalar_tensor_tensor(normed[:, u, SW:D].rearrange("p (c d) -> p c d", d=P),
                                         out_b[:, :, t * P:(t + 1) * P], rstd[:, NT + t:NT + t + 1],
                                         gain_pre[:, SW:D].rearrange("p (c d) -> p c d", d=P), ALU.mult, ALU.mult)\
                   .then_inc(merge["normed"], 1)

            copy_turned(N_ATT - 3)
            merge_tile(0)
            merge_tile(1)
            copy_turned(N_ATT - 1)
            out_b_tile(NT - 2)
            out_b_tile(NT - 1)
            for t in range(NT):
                turn_lo(dve, merge, t, x_hi, x_lo)
                if t + 2 < NT:
                    merge_tile(t + 2)
            dve.wait_ge(norm_mem["gains"], 16)
            dve.wait_ge(merge["turned"], NT)
            for t in range(NM):
                pre_norm(dve, norm_mem, t, resid_b[:, t, :], gain_post[:, :])
            next_lo(dve, uses, 0)
            next_lo(dve, uses, 1)
            for t in range(NM):
                turn_lo(dve, norm_mem, t, m_hi, m_lo)
            norm_and_split(dve, uses, norm2, True)
            for n in range(XK_BLOCKS + 4 + XK_BLOCKS - 3):
                next_lo(dve, uses, n % 2)

            def o_lo(t):
                dve.wait_ge(xatt["o_hi"], t + 1)
                at = slice(t * P, (t + 1) * P)
                dve.tensor_tensor(x_lo[:, :, at], bank(6, 2).rearrange("p (k c) -> p k c", c=P),
                                  x_hi[:, :, at].bitcast(F32), ALU.subtract).then_inc(xatt["o_full"], 1)

            for t in range(NT):
                u = t % 2
                m0, n0, r0, s0 = 32 + 4 * u, 48 + 4 * u, 40 + 4 * u, 56 + 4 * u
                dve.wait_ge(xatt["logits"], t + 1)
                if t >= 2:
                    dve.wait_ge(xatt["neg"], t - 1)
                dve.tensor_reduce(small[:, m0:m0 + 4], logits_bank(t).rearrange("p (h m) -> p h m", m=M), AX.X, ALU.max)\
                   .then_inc(xatt["max"], 1)
                dve.wait_ge(xatt["max"], t + 1)
                if t >= 2:
                    dve.wait_ge(xatt["probs"], XHEADS * (t - 1))
                dve.tensor_scalar(small[:, n0:n0 + 4], small[:, m0:m0 + 4], -(XHD ** -0.5), None, ALU.mult)\
                   .then_inc(xatt["neg"], 1)
                dve.wait_ge(xatt["probs"], XHEADS * (t + 1))
                if t >= 2:
                    dve.wait_ge(xatt["scaled"], XHEADS * (t - 1))
                dve.reciprocal(small[:, r0:r0 + 4], small[:, s0:s0 + 4]).then_inc(xatt["recip"], 1)
                dve.wait_ge(xatt["recip"], t + 1)
                for h in range(XHEADS):
                    dve.tensor_scalar(probs[:, u, h, :], probs[:, u, h, :], small[:, r0 + h:r0 + h + 1], None,
                                      ALU.mult).then_inc(xatt["scaled"], 1)
                if t >= 1:
                    o_lo(t - 1)
                dve.wait_ge(xatt["turned"], t + 1)
                dve.tensor_copy(probs_t[:, :], bank(4, 2)).then_inc(xatt["probs_t"], 1)
                if t == 1:
                    next_lo(dve, uses, 1)
            o_lo(NT - 1)
            next_lo(dve, uses, 0)
            next_lo(dve, uses, 1)
            norm_and_split(dve, uses, norm3, False)

            def h_stored():
                for u in range(2):
                    dve.wait_ge(norm3[f"stored{u}"], 16 * PAIRS)

            def ffn2_end(hidden3, add):
                for t in range(3):
                    add(t)
                post_norm(dve, norm4, 0, 0.5, resid_a)
                post_norm(dve, norm4, 1, 0.5, resid_a)
                post_norm(dve, norm4, 2, 0.5, resid_a)
                hidden3()
                add(3)
                for t in range(3, NT):
                    if t + 1 < NT:
                        add(t + 1)
                    post_norm(dve, norm4, t, 0.5, resid_a)
                for t in range(NT - 2, NT):
                    dve.wait_ge(norm4["rstd_h"], t + 1)
                    dve.scalar_tensor_tensor(y[:, t, :], y[:, t, :], rstd[:, NT + t:NT + t + 1], gain_pre[:, :],
                                             ALU.mult, ALU.mult).then_inc(norm4["last_normed"], 1)

            ffn_dve(dve, uses, CHUNKS, h_stored, ffn2_end)

        def split3(pe, dst, lh, ll, rh, rl, first, last):
            pe.matmul(dst, lh, rh, start=first, stop=False)
            pe.matmul(dst, lh, rl, start=False, stop=False)
            return pe.matmul(dst, ll, rh, start=False, stop=last)

        def turn(pe, s, t):
            pe.wait_ge(s["normed"], t + 1)
            if t >= 2:
                pe.wait_ge(s["x_full"], t - 1)
            for k in range(NK):
                mm = pe.transpose(turn_bank(t)[:, k * P:(k + 1) * P], normed[:, t % 2, k * P:(k + 1) * P], ident[:, :])
            mm.then_inc(s["turned"], 1)

        def rows_part(pe, b, t, s, src_hi, src_lo):
            for k in range(4):
                kk = 4 * s + k
                mm = split3(pe, bank(b), src_hi[:, kk, t * P:(t + 1) * P], src_lo[:, kk, t * P:(t + 1) * P],
                            hi(s)[:, k * BANK:(k + 1) * BANK], lo(s)[:, k * BANK:(k + 1) * BANK],
                            s == 0 and k == 0, s == 1 and k == 3)
            return mm

        def rows_pair(pe, uses, st, p, tiles, banks, wait, between):
            a_, b_ = tiles
            last = p == "last"
            for s in range(2):
                pe.wait_ge(w_full[s], uses.n[s] + 1)
                for j, t in enumerate((a_, b_)):
                    if s == 0:
                        wait(t)
                    mm = rows_part(pe, banks[j], t, s, *st["src"])
                    if s == 0 and j == 1 and last:
                        mm.then_inc(st["half"], 1)
                    if s == 1:
                        mm.then_inc(st["full"], 1)
                    between(2 * s + j)
            if last:
                for s in range(2):
                    uses.n[s] += 1

        def ffn_pe(pe, uses, c0, x_full, banks_free, between, turn_late):
            def gate_up_part(i, first, q):
                f, h = q % 2, q // 2
                if q < 2:
                    pe.wait_ge(w_full[f], uses.n[f] + 1 - c0 + i)
                if first and q % 2 == 0:
                    pe.wait_ge(x_full, NT // 2 * (h + 1))
                if first and q == 0:
                    banks_free()
                if not (first and q < 2):
                    pe.wait_ge(ffn["product"], 4 * i + q - 1)
                for g in range(2):
                    for k in range(NK):
                        at = slice((g * NK + k) * P, (g * NK + k + 1) * P)
                        half = slice(h * HALF, (h + 1) * HALF)
                        mm = split3(pe, bank(2 * (q % 2) + g), hi(f)[:, at], lo(f)[:, at],
                                    x_hi[:, k, half], x_lo[:, k, half], k == 0, k == NK - 1)
                    mm.then_inc(ffn["gu"], 1)
                    if first:
                        between(2 * q + g)

            def down_part(i, first, last, t):
                for h in range(2):
                    n = 2 * t + h
                    b = last_bank(c0, n) if last else 4 + n % 4
                    if last and 6 <= n < 10:
                        if n % 2 == 0:
                            pe.wait_ge(ffn["product"], 4 * i + n // 2)
                    elif last and c0 and n >= 10:
                        if n not in (12, 13):
                            pe.wait_ge(ffn["y"], 2 * NT * i + (n - 5 if n < 12 else n - 7))
                    elif not (first and n < 4):
                        pe.wait_ge(ffn["y"], 2 * NT * i + n - 3)
                    for f in range(2):
                        at = slice(f * D + h * BANK, f * D + (h + 1) * BANK)
                        mm = split3(pe, bank(b), hid_hi[:, f, t * P:(t + 1) * P],
                                    hid_lo[:, f, t * P:(t + 1) * P], w2_hi[:, at], w2_lo[:, at], f == 0, f == 1)
                    mm.then_inc(ffn["down"], 1)

            def chunk(i, first, last):
                for q in range(4):
                    if last and q == 3:
                        pe.wait_ge(w_full[2], i + 1)
                        pe.wait_ge(ffn["hid_full"], 4 * i + 2)
                        for t in range(3):
                            down_part(i, first, last, t)
                    gate_up_part(i, first, q)
                    if last and q == 3:
                        turn_late(0)
                if not last:
                    pe.wait_ge(w_full[2], i + 1)
                    pe.wait_ge(ffn["hid_full"], 4 * i + 2)
                for t in range(3 if last else 0, NT):
                    if t == NT // 2:
                        pe.wait_ge(ffn["hid_full"], 4 * i + 4)
                    down_part(i, first, last, t)
                    if last:
                        turn_late(t)

            chunk(c0, True, False)
            with pe.Fori(c0 + 1, c0 + CHUNKS - 1) as i:
                chunk(i, False, False)
            chunk(c0 + CHUNKS - 1, False, True)
            for f in range(3):
                uses.n[f] += CHUNKS

        def cols_group(pe, b, s, c, width, h, src_hi, src_lo):
            for k in range(NK):
                at = slice(k * COLS + c * P, k * COLS + (c + 1) * P)
                mm = split3(pe, bank(b)[:, 0:width], hi(s)[:, at], lo(s)[:, at],
                            src_hi[:, k, h * width:(h + 1) * width], src_lo[:, k, h * width:(h + 1) * width],
                            k == 0, k == NK - 1)
            return mm

        @block.tensor
        def _(pe):
            uses = Uses()
            nothing = lambda *_: None
            pe.wait_ge(own_result, CONSTANT_STEPS)
            for t in range(4):
                turn(pe, norm0, t)

            def x_turns(n):
                if n < 2:
                    turn(pe, norm0, 4 + 2 * n)
                    turn(pe, norm0, 5 + 2 * n)

            ffn_end = 2 * NT * (CHUNKS - 1)

            def norm1_turns(t):
                if t == 0:
                    pe.wait_ge(ffn["y"], ffn_end + 6)
                    turn(pe, norm1, 0)
                if t in (3, 6):
                    turn(pe, norm1, t // 3)

            ffn_pe(pe, uses, 0, norm0["x_full"], nothing, x_turns, norm1_turns)
            pe.wait_ge(ffn["y"], ffn_end + 16)

            def pairs(st, cb, wait, between=nothing):
                for p in range(PAIRS):
                    rows_pair(pe, uses, st, "last" if p == PAIRS - 1 else p, (2 * p, 2 * p + 1),
                              (2 * p % 4, 2 * p % 4 + 1), wait, lambda n: between(p, n))

            x_mix = {"src": (x_hi, x_lo), "half": mix["half"], "full": mix["full"]}

            def u_wait(t):
                pe.wait_ge(norm1["x_full"], t + 1)
                if t >= 4:
                    pe.wait_ge(mix["u"], t - 3)

            norm1_rest = {(0, 1): 3, (0, 3): 4, (1, 1): 5, (1, 3): 6, (2, 1): 7}

            def u_between(p, n):
                if (p, n) in norm1_rest:
                    turn(pe, norm1, norm1_rest[p, n])

            pairs(x_mix, 0, u_wait, u_between)
            pe.wait_ge(mix["masked"], 1)
            for g in range(G):
                mm = pe.transpose(bank(6)[:, g * P:(g + 1) * P], ws_raw[:, g, :], ident[:, :])
            mm.then_inc(mix["ws_turned"], 1)
            pairs(x_mix, 1, lambda t: pe.wait_ge(mix["u"], t + 5) if t < 4 else pe.wait_ge(mix["vg"], t - 3))

            def causal_mix(p, n):
                if n == 1 and p == 0:
                    pe.wait_ge(mix["ws"], 1)
                if n in (1, 3):
                    t = 2 * p + n // 2
                    pe.wait_ge(mix["vn"], t + 1)
                    if t >= 2:
                        pe.wait_ge(mix["out_a"], G * (t - 1))
                    for g in range(G):
                        at = slice(g * GD, (g + 1) * GD)
                        mm = pe.matmul(bank(4 + t % 2)[:, at], ws_t[:, g, :], vg[:, t, at], start=True, stop=True)
                    mm.then_inc(mix["mixed"], 1)

            pairs(x_mix, 2, lambda t: pe.wait_ge(mix["vg"], t + 5) if t < 4 else pe.wait_ge(mix["v_done"], t - 3),
                  causal_mix)
            for b in range(QK_BLOCKS):
                s = b % 2
                pe.wait_ge(w_full[s], uses.n[s] + 1)
                for n in range(4):
                    idx = 4 * b + n
                    if idx < 4:
                        pe.wait_ge(mix["v_done"], idx + 5)
                    else:
                        pe.wait_ge(mix["qk_done"], 2 * (idx - 3))
                    cols_group(pe, idx % 4, s, n // 2, BANK, n % 2, x_hi, x_lo).then_inc(mix["qk"], 1)
                uses.n[s] += 1

            def scores(n):
                i, h = att_step(n)
                W = (i + 1) * P
                if n >= 2:
                    pe.wait_ge(sb_att["keep"], n - 1)
                else:
                    pe.wait_ge(mix["qk_done"], 2 * (4 * QK_BLOCKS - 2 + 2 * n))
                q = (q_even, q_odd)[h % 2]
                z = bank(2 * (n % 2), 2)
                for c in range(0, W, BANK):
                    c1 = min(W, c + BANK)
                    mm = pe.matmul(z[:, c:c1], q[:, h // 2, i * P:(i + 1) * P], k_t[:, h // 2, c:c1],
                                   start=True, stop=c1 < W)
                pe.matmul(z[:, W - P:W], ident_bf[:, :], causal_neg[:, :], start=False, stop=True)\
                  .then_inc(sb_att["z"], 1)

            def turns(n):
                pe.wait_ge(sb_att["attn"], n + 1)
                if n >= 1:
                    pe.wait_ge(sb_att["attn_t"], n)
                for j in range(att_step(n)[0] + 1):
                    mm = pe.transpose(bank(4, 2)[:, j * P:(j + 1) * P], beta[:, n % 3, j * P:(j + 1) * P], ident[:, :])
                mm.then_inc(sb_att["turned"], 1)

            def values(n):
                i, h = att_step(n)
                pe.wait_ge(sb_att["attn_t"], n + 1)
                if h == 0 and n >= PAIR_STEPS:
                    pe.wait_ge(sb_att["out_b"], 2 * (n // PAIR_STEPS))
                for j in range(i + 1):
                    mm = pe.matmul(bank(6 + i % 2)[:, h * HD:(h + 1) * HD], attn_t[:, n % 2, j * P:(j + 1) * P],
                                   v_sb[:, j, h * HD:(h + 1) * HD], start=j == 0, stop=j == i)
                mm.then_inc(sb_att["av"], 1)

            pe.wait_ge(mix["padded"], 2)
            pe.wait_ge(mix["out_a"], G * NT)
            scores(0)
            for n in range(N_ATT + 3):
                if n + 1 < N_ATT:
                    scores(n + 1)
                if 2 <= n < N_ATT + 2:
                    turns(n - 2)
                if n >= 3:
                    values(n - 3)

            turn(pe, merge, 0)
            pe.wait_ge(sb_att["out_b"], NT)
            turn(pe, merge, 1)

            def wout_between(p, n):
                if 4 * p + n < NT - 2:
                    turn(pe, merge, 4 * p + n + 2)
                if p == PAIRS - 1 and n in (1, 2):
                    if n == 1:
                        pe.wait_ge(merge["x_full"], NT)
                    turn(pe, norm_mem, n - 1)

            x_wout = {"src": (x_hi, x_lo), "half": wout["half"], "full": wout["full"]}

            def wout_wait(t):
                pe.wait_ge(merge["x_full"], t + 1)
                if t >= 4:
                    pe.wait_ge(wout["y"], t - 3)

            pairs(x_wout, 0, wout_wait, wout_between)

            def ahead(s, p, n):
                if n == 3 and p > 0:
                    if s is norm2 and p == 1:
                        pe.wait_ge(norm_mem["x_full"], NM)
                    for t in (2 * p - 2, 2 * p - 1):
                        turn(pe, s, t)

            pairs(x_wout, 1, lambda t: pe.wait_ge(wout["y"], NT + t - 3), lambda p, n: ahead(norm2, p, n))

            for b in range(XK_BLOCKS):
                s = b % 2
                pe.wait_ge(w_full[s], uses.n[s] + 1)
                for c in range(2):
                    idx = 2 * b + c
                    if idx < 4:
                        pe.wait_ge(wout["y"], 2 * NT - 3 + idx)
                    else:
                        pe.wait_ge(xkv["k_done"], idx - 3)
                    cols_group(pe, idx % 4, s, c, M, 0, m_hi, m_lo).then_inc(xkv["k"], 1)
                    if idx in (4, 5):
                        turn(pe, norm2, NT - 6 + idx)
                uses.n[s] += 1
            x_mem = {"src": (m_hi, m_lo), "half": xkv["half"], "full": xkv["v"]}
            for cb in range(2):
                rows_pair(pe, uses, x_mem, "last", (0, 1), (2 * cb, 2 * cb + 1),
                          lambda t: pe.wait_ge(xkv["k_done"], 2 * XK_BLOCKS - 3 + 2 * cb + t), nothing)
            pe.wait_ge(norm2["x_full"], NT)
            for b in range(XK_BLOCKS):
                s = b % 2
                pe.wait_ge(w_full[s], uses.n[s] + 1)
                for n in range(4):
                    idx = 4 * b + n
                    if idx < 4:
                        pe.wait_ge(xkv["v_done"], idx + 1)
                    else:
                        pe.wait_ge(xq["q_done"], idx - 3)
                    cols_group(pe, idx % 4, s, n // 2, BANK, n % 2, x_hi, x_lo).then_inc(xq["q"], 1)
                uses.n[s] += 1

            def logits(t):
                if t == 0:
                    pe.wait_ge(xq["q_done"], 4 * XK_BLOCKS)
                elif t > 1:
                    pe.wait_ge(xatt["probs"], XHEADS * t)
                for h in range(XHEADS):
                    for c in range(2):
                        mm = pe.matmul(logits_bank(t)[:, h * M:(h + 1) * M], xq_t[:, 2 * h + c, t * P:(t + 1) * P],
                                       mem_k[:, 2 * h + c, :], start=c == 0, stop=c == 1)
                mm.then_inc(xatt["logits"], 1)

            def turn_probs(t):
                pe.wait_ge(xatt["scaled"], XHEADS * (t + 1))
                if t >= 1:
                    pe.wait_ge(xatt["probs_t"], t)
                for n in range(XHEADS * NM):
                    h, m = divmod(n, NM)
                    mm = pe.transpose(bank(4, 2)[:, n * P:(n + 1) * P], probs[:, t % 2, h, m * P:(m + 1) * P], ident[:, :])
                mm.then_inc(xatt["turned"], 1)

            def mem_values(t):
                pe.wait_ge(xatt["probs_t"], t + 1)
                if t >= 1:
                    pe.wait_ge(xatt["o_full"], t)
                for k in range(NK):
                    h = k // (NK // XHEADS)
                    for m in range(NM):
                        mm = pe.matmul(bank(6, 2)[:, k * P:(k + 1) * P], mem_v[:, m, k * P:(k + 1) * P],
                                       probs_t[:, (h * NM + m) * P:(h * NM + m + 1) * P], start=m == 0, stop=m == NM - 1)
                mm.then_inc(xatt["o"], 1)

            def project_o(t, s):
                if t == 0:
                    pe.wait_ge(w_full[s], uses.n[s] + 1)
                if s == 0:
                    pe.wait_ge(xatt["o_full"], t + 1)
                    if t >= 2:
                        pe.wait_ge(xo["y"], t - 1)
                mm = rows_part(pe, 2 + t % 2, t, s, x_hi, x_lo)
                if s == 0 and t == NT - 1:
                    mm.then_inc(xo["half"], 1)
                if s == 1:
                    mm.then_inc(xo["full"], 1)

            logits(0)
            for t in range(NT):
                if t + 1 < NT:
                    logits(t + 1)
                if t >= 2:
                    project_o(t - 2, 0)
                turn_probs(t)
                if t >= 2:
                    project_o(t - 2, 1)
                mem_values(t)
            for s in range(2):
                for t in (NT - 2, NT - 1):
                    project_o(t, s)
            for s in range(2):
                uses.n[s] += 1
            x_xo = {"src": (x_hi, x_lo), "half": xo["half"], "full": xo["full"]}

            def xo_wait(t):
                if t >= 2:
                    pe.wait_ge(xo["y"], NT + t - 3)

            pairs(x_xo, 1, xo_wait, lambda p, n: ahead(norm3, p, n))

            def norm3_turns(n):
                if n in (1, 2):
                    turn(pe, norm3, NT - 3 + n)

            ffn_pe(pe, uses, CHUNKS, norm3["x_full"], lambda: pe.wait_ge(xo["y"], 2 * NT), norm3_turns, nothing)


_INS = ["x", "mem", "ffn1_pre_g", "ffn1_post_g", "ffn1_w_gate", "ffn1_w_up", "ffn1_w_down", "mix_pre_g",
        "mix_post_g", "w_in", "sgu_norm_g", "sgu_norm_b", "sgu_w_s", "sgu_b_s", "sgu_out_g", "sb_out_g", "w_out",
        "xa_pre_g", "xa_post_g", "mem_norm_g", "xa_w_q", "xa_w_kv", "xa_w_o", "ffn2_pre_g", "ffn2_post_g",
        "ffn2_w_gate", "ffn2_w_up", "ffn2_w_down", "final_norm_g"]


def kernel(**inputs):
    import numpy as _np
    import concourse.bacc as _bacc
    from concourse import mybir as _mybir
    from concourse.bass_utils import run_bass_kernel_spmd as _run

    nc = _bacc.Bacc("TRN2", target_bir_lowering=False, num_devices=1)
    arrays, args = {}, {}
    for name in _INS:
        v = _np.ascontiguousarray(inputs[name])
        arrays[f"in_{name}"] = v
        args[name] = nc.dram_tensor(f"in_{name}", v.shape, _mybir.dt.from_np(v.dtype), kind="ExternalInput").ap()
    out = nc.dram_tensor("out_0", inputs["x"].shape, _mybir.dt.float32, kind="ExternalOutput").ap()
    build(nc, args, out)
    r = _run(nc, [arrays], core_ids=[0])
    return r.results[0]["out_0"]
```
